# Optimizing a Trainium2 kernel written in Bass

```python
import jax, jax.numpy as jnp
from jax import lax
import numpy as np

D_MODEL = 1024
BATCH = 1
SEQ = 2048
DEPTH = 1

HEAD_DIM = 64
A_HEADS = D_MODEL // (2 * HEAD_DIM)
B_HEADS = D_MODEL // (2 * HEAD_DIM)
A_WIDTH = A_HEADS * HEAD_DIM
B_WIDTH = B_HEADS * HEAD_DIM
MIX_WIDTH = A_WIDTH + B_WIDTH
IN_WIDTH = 2 * A_WIDTH + 3 * B_WIDTH
CHUNK = 128
DILATED_BRANCHES = ((128, 1), (512, 4), (2048, 16))
BAND_BLOCK = 128
ROPE_THETA = 10000.0
N_EXPERTS = 32
TOP_K = 4
D_FF = D_MODEL
SWIGLU_ALPHA = 1.702
SWIGLU_LIMIT = 7.0
NORM_EPS = 1e-5
NEG_INF = -1e30

kernel_name = "hymba_gmlp_dilated_moe_block"

def _rmsnorm(x, g):
    xf = x.astype(jnp.float32)
    y = xf * lax.rsqrt(jnp.mean(xf * xf, axis=-1, keepdims=True) + NORM_EPS)
    return (y * g.astype(jnp.float32)).astype(x.dtype)

def _rope_tables(s):
    pos = jnp.arange(s, dtype=jnp.float32)
    inv = ROPE_THETA ** (-jnp.arange(0, HEAD_DIM, 2, dtype=jnp.float32) / HEAD_DIM)
    ang = pos[:, None] * inv[None, :]
    emb = jnp.concatenate([ang, ang], axis=-1)
    return jnp.cos(emb), jnp.sin(emb)

def _apply_rope(t, cos, sin):
    tf = t.astype(jnp.float32)
    half = HEAD_DIM // 2
    rot = jnp.concatenate([-tf[..., half:], tf[..., :half]], axis=-1)
    return (tf * cos[:, None, :] + rot * sin[:, None, :]).astype(t.dtype)

def _spatial_gating(u, v, ln_g, ln_b, w_s, b_s):
    b, s, h, dh = v.shape
    u = jax.nn.gelu(u.astype(jnp.float32))
    vf = jax.nn.gelu(v.astype(jnp.float32))
    mu = jnp.mean(vf, axis=-1, keepdims=True)
    var = jnp.mean(jnp.square(vf - mu), axis=-1, keepdims=True)
    vn = (vf - mu) * lax.rsqrt(var + NORM_EPS) * ln_g.astype(jnp.float32) + ln_b.astype(jnp.float32)
    nc = s // CHUNK
    vn = vn.reshape(b, nc, CHUNK, h, dh)
    causal = jnp.tril(jnp.ones((CHUNK, CHUNK), dtype=bool))
    ws = jnp.where(causal[None], w_s.astype(jnp.float32), 0.0)
    g = jnp.einsum('hts,bnshd->bnthd', ws, vn) + b_s.astype(jnp.float32).T[:, :, None]
    return u * g.reshape(b, s, h, dh)

def _dilated_branch(q, k, v, steps, dil, scale):
    b, h, s, dh = q.shape
    L = s // dil
    nb = -(-L // BAND_BLOCK)
    Lp = nb * BAND_BLOCK

    def split(t):
        t = t.reshape(b, h, L, dil, dh).transpose(0, 1, 3, 2, 4)
        t = jnp.pad(t, ((0, 0), (0, 0), (0, 0), (0, Lp - L), (0, 0)))
        return t.reshape(b, h, dil, nb, BAND_BLOCK, dh)

    def with_prev(t):
        prev = jnp.concatenate([jnp.zeros_like(t[:, :, :, :1]), t[:, :, :, :-1]], axis=3)
        return jnp.concatenate([prev, t], axis=4)

    qb = split(q)
    kw = with_prev(split(k))
    vw = with_prev(split(v))
    sc = jnp.einsum('bhrnqd,bhrnkd->bhrnqk', qb, kw,
                    preferred_element_type=jnp.float32) * scale
    qpos = jnp.arange(BAND_BLOCK)[:, None] + BAND_BLOCK
    kpos = jnp.arange(2 * BAND_BLOCK)[None, :]
    rel = qpos - kpos
    band = (rel >= 0) & (rel <= steps)
    not_first = (jnp.arange(nb) > 0)[:, None, None]
    mask = band[None] & (not_first | (kpos >= BAND_BLOCK)[None])
    sc = jnp.where(mask, sc, NEG_INF)
    m = jnp.max(sc, axis=-1, keepdims=True)
    p = jnp.exp(sc - m)
    l = jnp.sum(p, axis=-1, keepdims=True)
    o = jnp.einsum('bhrnqk,bhrnkd->bhrnqd', p, vw.astype(jnp.float32)) / l
    lse = (m + jnp.log(l))[..., 0]
    o = o.reshape(b, h, dil, Lp, dh)[:, :, :, :L].transpose(0, 1, 3, 2, 4).reshape(b, h, s, dh)
    lse = lse.reshape(b, h, dil, Lp)[..., :L].transpose(0, 1, 3, 2).reshape(b, h, s)
    return o, lse

def _dilated_mixture(q, k, v):
    scale = HEAD_DIM ** -0.5
    outs, lses = [], []
    for window, dil in DILATED_BRANCHES:
        o, lse = _dilated_branch(q, k, v, window // dil, dil, scale)
        outs.append(o)
        lses.append(lse)
    w = jax.nn.softmax(jnp.stack(lses), axis=0)
    return jnp.einsum('nbhs,nbhsd->bhsd', w, jnp.stack(outs))

def _moe(xn, w_router, b_router, w_gate_up, b_gate_up, w_down, b_down):
    b, s, d = xn.shape
    xf = xn.reshape(-1, d)
    t = xf.shape[0]
    logits = jnp.dot(xf, w_router, preferred_element_type=jnp.float32) + b_router.astype(jnp.float32)
    top_val, top_idx = lax.top_k(logits, TOP_K)
    gates = jax.nn.softmax(top_val, axis=-1)
    flat_e = top_idx.reshape(-1)
    order = jnp.argsort(flat_e)
    e_sorted = flat_e[order]
    tok = order // TOP_K
    gate_sorted = gates.reshape(-1)[order]
    group_sizes = jnp.bincount(flat_e, length=N_EXPERTS).astype(jnp.int32)
    xs = xf[tok]
    hgu = lax.ragged_dot(xs, w_gate_up, group_sizes) + b_gate_up[e_sorted]
    gate = jnp.minimum(hgu[:, :D_FF], SWIGLU_LIMIT)
    up = jnp.clip(hgu[:, D_FF:], -SWIGLU_LIMIT, SWIGLU_LIMIT)
    act = (up + 1) * (gate * jax.nn.sigmoid(gate * SWIGLU_ALPHA))
    y = lax.ragged_dot(act, w_down, group_sizes) + b_down[e_sorted]
    y = y * gate_sorted[:, None].astype(y.dtype)
    out = jnp.zeros((t, d), y.dtype).at[tok].add(y)
    return out.reshape(b, s, d).astype(xn.dtype)

def setup_inputs(seed: int = 0) -> dict:
    key = jax.random.key(seed)
    ks = jax.random.split(key, 20)
    f32 = jnp.float32
    n = lambda k, shape, sc: jax.random.normal(k, shape, f32) * sc
    return {
        "x": jax.random.normal(ks[0], (BATCH, SEQ, D_MODEL), f32),
        "norm1_g": 1.0 + n(ks[1], (DEPTH, D_MODEL), 0.02),
        "w_in": n(ks[2], (DEPTH, D_MODEL, IN_WIDTH), D_MODEL ** -0.5),
        "a_ln_g": 1.0 + n(ks[3], (DEPTH, A_HEADS, HEAD_DIM), 0.02),
        "a_ln_b": n(ks[4], (DEPTH, A_HEADS, HEAD_DIM), 0.02),
        "a_w_s": n(ks[5], (DEPTH, A_HEADS, CHUNK, CHUNK), CHUNK ** -0.5),
        "a_b_s": 1.0 + n(ks[6], (DEPTH, A_HEADS, CHUNK), 0.02),
        "a_out_g": 1.0 + n(ks[7], (DEPTH, A_WIDTH), 0.02),
        "b_out_g": 1.0 + n(ks[8], (DEPTH, B_WIDTH), 0.02),
        "w_out": n(ks[9], (DEPTH, MIX_WIDTH, D_MODEL), MIX_WIDTH ** -0.5),
        "norm2_g": 1.0 + n(ks[10], (DEPTH, D_MODEL), 0.02),
        "w_router": n(ks[11], (DEPTH, D_MODEL, N_EXPERTS), D_MODEL ** -0.5),
        "b_router": n(ks[12], (DEPTH, N_EXPERTS), 0.01),
        "w_gate_up": n(ks[13], (DEPTH, N_EXPERTS, D_MODEL, 2 * D_FF), D_MODEL ** -0.5),
        "b_gate_up": n(ks[14], (DEPTH, N_EXPERTS, 2 * D_FF), 0.01),
        "w_down": n(ks[15], (DEPTH, N_EXPERTS, D_FF, D_MODEL), D_FF ** -0.5),
        "b_down": n(ks[16], (DEPTH, N_EXPERTS, D_MODEL), 0.01),
        "normf_g": 1.0 + n(ks[17], (D_MODEL,), 0.02),
    }

def reference(x, norm1_g, w_in, a_ln_g, a_ln_b, a_w_s, a_b_s, a_out_g, b_out_g, w_out,
              norm2_g, w_router, b_router, w_gate_up, b_gate_up, w_down, b_down, normf_g):
    b, s, _ = x.shape
    cos, sin = _rope_tables(s)
    cuts = [A_WIDTH, 2 * A_WIDTH, 2 * A_WIDTH + B_WIDTH, 2 * A_WIDTH + 2 * B_WIDTH]
    h = x
    for layer in range(DEPTH):
        xn = _rmsnorm(h, norm1_g[layer])
        proj = jnp.einsum('bsd,de->bse', xn, w_in[layer])
        a_u, a_v, q, k, v = jnp.split(proj, cuts, axis=-1)
        a_out = _spatial_gating(a_u.reshape(b, s, A_HEADS, HEAD_DIM),
                                a_v.reshape(b, s, A_HEADS, HEAD_DIM),
                                a_ln_g[layer], a_ln_b[layer], a_w_s[layer], a_b_s[layer])
        a_out = _rmsnorm(a_out.reshape(b, s, A_WIDTH), a_out_g[layer])
        q = _apply_rope(q.reshape(b, s, B_HEADS, HEAD_DIM), cos, sin).transpose(0, 2, 1, 3)
        k = _apply_rope(k.reshape(b, s, B_HEADS, HEAD_DIM), cos, sin).transpose(0, 2, 1, 3)
        v = v.reshape(b, s, B_HEADS, HEAD_DIM).transpose(0, 2, 1, 3)
        b_out = _dilated_mixture(q, k, v).transpose(0, 2, 1, 3).reshape(b, s, B_WIDTH)
        b_out = _rmsnorm(b_out, b_out_g[layer])
        mixed = jnp.concatenate([a_out, b_out], axis=-1).astype(h.dtype)
        h = h + jnp.einsum('bse,ed->bsd', mixed, w_out[layer])
        hn = _rmsnorm(h, norm2_g[layer])
        h = h + _moe(hn, w_router[layer], b_router[layer], w_gate_up[layer],
                     b_gate_up[layer], w_down[layer], b_down[layer])
    return _rmsnorm(h, normf_g)


_drawn_inputs = setup_inputs


def setup_inputs(seed=0):
    import zlib

    import numpy as np

    out = dict(_drawn_inputs(seed))
    spreads = {}
    factors = {'a_ln_g': 3.424,
     'a_ln_b': 3.535,
     'a_b_s': 2.672,
     'b_router': 2.797,
     'b_gate_up': 8.0,
     'b_down': 8.0,
     'normf_g': 2.877}
    for name, (base, spread) in spreads.items():
        noise = np.random.default_rng([zlib.crc32(name.encode()), seed]).standard_normal(out[name].shape)
        drawn = base * np.exp(spread * noise) if base else spread * noise
        out[name] = __import__('jax').numpy.asarray(drawn.astype(out[name].dtype))
    for name, factor in factors.items():
        out[name] = (out[name] * factor).astype(out[name].dtype)
    return out
```

```python
from contextlib import ExitStack

import concourse.bass as bass
from concourse import mybir

F32 = mybir.dt.float32
F32R = mybir.dt.float32r
BF16 = mybir.dt.bfloat16
I32 = mybir.dt.int32
U32 = mybir.dt.uint32
ALU = mybir.AluOpType
ACT = mybir.ActivationFunctionType
AX = mybir.AxisListType

P = 128
S = 2048
D = 1024
T = S // P
KD = D // P
H = 8
DH = 64
W = H * DH
PAIRS = H // 2
E = 32
TOPK = 4
FF = D
SLOT = 512
ST = SLOT // P
NSLOTS = (S * TOPK + E * (SLOT - 1)) // SLOT
EPS = 1e-5
SCALE = DH ** -0.5
ALPHA = 1.702
LIMIT = 7.0
OROW = W + 2 * H
DILATIONS = (1, 4, 16)
LIST_ROWS = (NSLOTS + 1) * SLOT
LROW = 16
SPLIT3 = ((0, 0), (0, 1), (1, 0))


def stage_semaphores(nc, ctx, name):
    used = []

    def clear():
        nc.clear_and_free_semaphores(used)
        nc.all_engine_barrier()

    def sem(s):
        used.append(nc.alloc_semaphore(f"{name}_{s}"))
        return used[-1]

    ctx.callback(clear)
    return sem


def wait(eng, sem, value):
    if not isinstance(value, int) or value > 0:
        eng.wait_ge(sem, value)


class Chain:

    def __init__(self, eng, sem, base):
        self.eng, self.sem, self.base, self.n = eng, sem, base, 0

    def then(self, ins):
        ins.then_inc(self.sem, 1)
        self.n += 1
        self.eng.wait_ge(self.sem, self.base + self.n)


ROOT_STEPS = 10
ROOT_WORK = 4
ROOT_GUESS = 0x5F3759DF


def inverse_root(nc, chain, value, sums, work, out):
    v = nc.vector
    mean, neg_half, t, y = (work[:, n, :] for n in range(4))
    chain.then(v.tensor_scalar(mean, sums, value, EPS, ALU.mult, ALU.add))
    v.tensor_scalar(neg_half, mean, -0.5, None, ALU.mult)
    chain.then(v.tensor_scalar(y.bitcast(I32), mean.bitcast(I32), -0.5, float(ROOT_GUESS), ALU.mult, ALU.add))
    for turn in range(3):
        chain.then(v.tensor_tensor(t, y, y, ALU.mult))
        chain.then(v.tensor_tensor(t, t, neg_half, ALU.mult))
        last = v.scalar_tensor_tensor(out if turn == 2 else y, t, 1.5, y, ALU.add, ALU.mult)
        if turn < 2:
            chain.then(last)
    assert chain.n == ROOT_STEPS
    return last


class Tile:

    def __init__(self, i, p):
        self.i, self.p, self.t = i, p, 2 * i + p
        self.rows = bass.ds(self.t * P, P)

    def has(self, d):
        return not isinstance(self.t, int) or 0 <= self.t + d < T

    def at(self, d):
        j = self.p + d
        return Tile(self.i + j // 2, j % 2)


def over_tiles(eng, body, ahead=2):
    last = T // 2 - (ahead + 1) // 2
    for p in range(2):
        body(Tile(0, p))
    with eng.Fori(1, last) as i:
        for p in range(2):
            body(Tile(i, p))
    for i in range(last, T // 2):
        for p in range(2):
            body(Tile(i, p))


class Front:

    def __init__(self, nc, ctx, sem, name, keep, g_cols, w_dram, groups, rows=None):
        self.nc, self.w_dram, self.groups, self.ident = nc, w_dram, groups, keep["ident"]
        sb = lambda s, shape, dt=F32: ctx.enter_context(nc.sbuf_tensor(f"{name}_{s}", shape, dt))
        n = len(groups)
        self.xn = [sb("xn", [P, D])] * 2 if rows is None else rows
        self.xT = [sb(f"xT{p}", [P, 2, KD, P], F32R) for p in range(2)]
        self.raw = [sb(f"raw{r}", [P, KD, W]) for r in range(2)]
        self.w = [sb(f"w{g}", [P, 2, KD, W], F32R) for g in range(n)]
        self.g = sb("g", [P, KD])
        self.psT = ctx.enter_context(nc.psum_tensor(f"{name}_psT", [P, KD, P], F32))
        self.g_dram = g_cols
        self.g_in = sem("g_in")
        self.raw_in = [sem(f"raw_in{g}") for g in range(n)]
        self.w_hi, self.w_lo = sem("w_hi"), sem("w_lo")
        self.xn_ready = sem("xn_ready")
        self.turned = sem("turned")
        self.hi_ready, self.lo_ready = sem("hi_ready"), sem("lo_ready")
        self.gemm_done = sem("gemm_done")

    def load_weights(self, sp):
        sp.dma_start(self.g[:], self.g_dram).then_inc(self.g_in, 16)
        for n, c0 in enumerate(self.groups):
            if n >= 2:
                sp.wait_ge(self.w_lo, n - 1)
            sp.dma_start(self.raw[n % 2][:], self.w_dram[:, c0:c0 + W].rearrange("(k p) n -> p k n", p=P)
                         ).then_inc(self.raw_in[n], 16)

    def weights_hi(self, act):
        for n in range(len(self.groups)):
            act.wait_ge(self.raw_in[n], 16)
            self.nc.scalar.copy(self.w[n][:, 0], self.raw[n % 2][:]).then_inc(self.w_hi, 1)

    def hi_x(self, act, tile):
        act.wait_ge(self.turned, tile.t + 1)
        wait(act, self.gemm_done, tile.t - 1)
        for k in range(KD):
            ins = self.nc.scalar.mul(self.xT[tile.p][:, 0, k, :], self.psT[:, k, :], self.g[:, k:k + 1])
        ins.then_inc(self.hi_ready, 1)

    def weights_lo(self, dve):
        for n in range(len(self.groups)):
            dve.wait_ge(self.w_hi, n + 1)
            self.nc.vector.tensor_tensor(self.w[n][:, 1], self.raw[n % 2][:], self.w[n][:, 0].bitcast(F32),
                                         ALU.subtract).then_inc(self.w_lo, 1)

    def lo_x(self, dve, tile):
        dve.wait_ge(self.hi_ready, tile.t + 1)
        for k in range(KD):
            ins = self.nc.vector.scalar_tensor_tensor(
                self.xT[tile.p][:, 1, k, :], self.psT[:, k, :], self.g[:, k:k + 1],
                self.xT[tile.p][:, 0, k, :].bitcast(F32), ALU.mult, ALU.subtract)
        ins.then_inc(self.lo_ready, 1)

    def turn_x(self, pe, tile):
        pe.wait_ge(self.xn_ready, tile.t + 1)
        wait(pe, self.lo_ready, tile.t)
        for k in range(KD):
            ins = pe.transpose(self.psT[:, k, :], self.xn[tile.p][:, k * P:(k + 1) * P], self.ident[:])
        ins.then_inc(self.turned, 1)

    def gemm(self, pe, tile, n, out):
        if isinstance(tile.t, int) and tile.t == 0:
            pe.wait_ge(self.w_lo, n + 1)
        m = 0
        for k in range(KD):
            for a, b in SPLIT3:
                ins = pe.matmul(out, self.xT[tile.p][:, a, k, :], self.w[n][:, b, k, :],
                                start=(m == 0), stop=(m == 3 * KD - 1))
                m += 1
        return ins


class NormFront(Front):

    def __init__(self, nc, ctx, sem, name, keep, x, g_cols, w_dram, groups):
        super().__init__(nc, ctx, sem, name, keep, g_cols, w_dram, groups)
        sb = lambda s, shape, dt=F32: ctx.enter_context(nc.sbuf_tensor(f"{name}_{s}", shape, dt))
        self.x = x
        self.xt = [sb(f"x{p}", [P, D]) for p in range(2)]
        self.squares = sb("squares", [P, D])
        self.stat, self.work = sb("stat", [P, 2, 2]), sb("work", [P, ROOT_WORK, 1])
        self.x_in = [sem(f"x_in{p}") for p in range(2)]
        self.rstd_ready = sem("rstd_ready")
        self.squares_ready, self.root_steps = sem("squares_ready"), sem("root_steps")

    def load_x(self, sp, tile):
        wait(sp, self.xn_ready, tile.t - 1)
        sp.dma_start(self.xt[tile.p][:], self.x[tile.rows, :]).then_inc(self.x_in[tile.p], 16)

    def scale_x(self, act, tile):
        act.wait_ge(self.rstd_ready, tile.t + 1)
        wait(act, self.turned, tile.t)
        self.nc.scalar.mul(self.xn[tile.p][:], self.xt[tile.p][:], self.stat[:, tile.p, 1:2]
                           ).then_inc(self.xn_ready, 1)

    def sum_squares(self, dve, tile):
        v, st, p = self.nc.vector, self.stat, tile.p
        dve.wait_ge(self.x_in[p], 16 * tile.i + 16)
        wait(dve, self.xn_ready, tile.t - 1)
        v.tensor_tensor_reduce(self.squares[:], self.xt[p][:], self.xt[p][:], 1.0, 0.0,
                               ALU.mult, ALU.add, st[:, p, 0:1]).then_inc(self.squares_ready, 1)

    def rstd(self, dve, tile):
        self.sum_squares(dve, tile)
        dve.wait_ge(self.squares_ready, tile.t + 1)
        inverse_root(self.nc, Chain(dve, self.root_steps, ROOT_STEPS * tile.t), 1.0 / D,
                     self.stat[:, tile.p, 0:1], self.work[:], self.stat[:, tile.p, 1:2]
                     ).then_inc(self.rstd_ready, 1)


def gating_stage(nc, io, scratch, keep):
    with ExitStack() as ctx:
        sb = lambda s, shape, dt=F32: ctx.enter_context(nc.sbuf_tensor(f"ga_{s}", shape, dt))
        ps = lambda s, shape: ctx.enter_context(nc.psum_tensor(f"ga_ps_{s}", shape, F32))
        sem = stage_semaphores(nc, ctx, "ga")
        AV, V, U = 0, 1, 2
        f = NormFront(nc, ctx, sem, "ga", keep, io["x"], io["norm1_g"], io["w_in"], (W, 4 * W, 0))
        ident = keep["ident"]
        gains, biases = sb("ln_g", [P, W]), sb("ln_b", [P, W])
        ws, tri, bs = sb("ws", [P, H, P]), sb("tri", [P, P]), sb("bs", [P, H])
        vg, vc, vq, vn = (sb(s, [P, H, DH]) for s in ("vg", "vc", "vq", "vn"))
        ug = [sb(f"ug{p}", [P, H, DH]) for p in range(2)]
        gt, a = sb("gt", [P, H, DH]), sb("a", [P, H, DH])
        an = [sb(f"an{p}", [P, W]) for p in range(2)]
        vo = [sb(f"vo{p}", [P, W]) for p in range(2)]
        ln, ast = sb("ln", [P, 4, H]), sb("ast", [P, 2])
        ln_work, a_work = sb("ln_work", [P, ROOT_WORK, H]), sb("a_work", [P, ROOT_WORK, 1])
        psG = [ps(f"g{n}", [P, W]) for n in range(3)]
        psM = ps("mix", [P, H, DH])

        ws_in, tri_in, bs_in, lng_in, lnb_in = (sem(s) for s in ("ws_in", "tri_in", "bs_in", "lng_in", "lnb_in"))
        ws_masked = sem("ws_masked")
        proj_done = sem("proj_done")
        vg_ready, vo_ready, ug_ready = sem("vg_ready"), sem("vo_ready"), sem("ug_ready")
        vn_ready, mixed, combined = sem("vn_ready"), sem("mixed"), sem("combined")
        a_ready, an_ready = sem("a_ready"), sem("an_ready")
        ln_steps, bias_added = sem("ln_steps"), sem("bias_added")
        ln_root_steps, ln_rstd_ready = sem("ln_root_steps"), sem("ln_rstd_ready")
        a_squares_ready, a_root_steps = sem("a_squares_ready"), sem("a_root_steps")
        an_out = [sem(f"an_out{p}") for p in range(2)]
        vo_out = [sem(f"vo_out{p}") for p in range(2)]
        block = ctx.enter_context(nc.Block())

        @block.sync
        def _(sp):
            f.load_x(sp, Tile(0, 0))
            f.load_x(sp, Tile(0, 1))
            f.load_weights(sp)
            sp.dma_start(ws[:], io["a_w_s"]).then_inc(ws_in, 16)
            sp.dma_start(tri[:], io["tri"]).then_inc(tri_in, 16)
            sp.dma_start(bs[:], io["a_b_s"]).then_inc(bs_in, 16)
            sp.dma_start(gains[:], io["a_ln_g"].to_broadcast([P, W])).then_inc(lng_in, 16)
            sp.dma_start(biases[:], io["a_ln_b"].to_broadcast([P, W])).then_inc(lnb_in, 16)
            with sp.Fori(1, T // 2) as i:
                for p in range(2):
                    f.load_x(sp, Tile(i, p))

        @block.tensor
        def _(pe):
            def gate(tile):
                pe.wait_ge(vn_ready, tile.t + 1)
                wait(pe, combined, tile.t)
                for h in range(H):
                    ins = pe.matmul(psM[:, h, :], ws[:, h, :], vn[:, h, :], start=True, stop=True)
                ins.then_inc(mixed, 1)

            def body(tile):
                if tile.has(1):
                    f.turn_x(pe, tile.at(1))
                pe.wait_ge(f.lo_ready, tile.t + 1)
                for n, read in ((AV, vg_ready), (V, vo_ready), (U, ug_ready)):
                    wait(pe, read, tile.t)
                    ins = f.gemm(pe, tile, n, psG[n][:])
                    ins.then_inc(proj_done if n != U else f.gemm_done, 1)
                if tile.has(-1):
                    gate(tile.at(-1))

            pe.wait_ge(keep["ident_in"], 16)
            f.turn_x(pe, Tile(0, 0))
            pe.wait_ge(ws_masked, 1)
            over_tiles(pe, body)
            gate(Tile(T // 2 - 1, 1))

        @block.scalar
        def _(act):
            def finish(tile):
                act.wait_ge(a_ready, tile.t + 1)
                wait(act, an_out[tile.p], 16 * tile.i)
                nc.scalar.mul(an[tile.p][:], a[:].rearrange("p h d -> p (h d)"), ast[:, 1:2]
                              ).then_inc(an_ready, 1)
                act.wait_ge(vo_ready, tile.t + 1)
                act.dma_start(scratch["v"][tile.rows, :], vo[tile.p][:]).then_inc(vo_out[tile.p], 16)
                act.wait_ge(an_ready, tile.t + 1)
                act.dma_start(scratch["a"][tile.rows, :], an[tile.p][:]).then_inc(an_out[tile.p], 16)

            def body(tile):
                p, t = tile.p, tile.t
                if tile.has(1):
                    f.hi_x(act, tile.at(1))
                act.wait_ge(proj_done, 2 * t + 1)
                wait(act, vn_ready, t)
                nc.scalar.activation(vg[:].rearrange("p h d -> p (h d)"), psG[AV][:], ACT.Gelu_apprx_tanh
                                     ).then_inc(vg_ready, 1)
                act.wait_ge(proj_done, 2 * t + 2)
                wait(act, vo_out[p], 16 * tile.i)
                nc.scalar.copy(vo[p][:], psG[V][:]).then_inc(vo_ready, 1)
                act.wait_ge(f.gemm_done, t + 1)
                wait(act, combined, t - 1)
                nc.scalar.activation(ug[p][:].rearrange("p h d -> p (h d)"), psG[U][:], ACT.Gelu_apprx_tanh
                                     ).then_inc(ug_ready, 1)
                if tile.has(-1):
                    finish(tile.at(-1))
                if tile.has(2):
                    f.scale_x(act, tile.at(2))

            act.wait_ge(f.g_in, 16)
            f.scale_x(act, Tile(0, 0))
            f.hi_x(act, Tile(0, 0))
            f.scale_x(act, Tile(0, 1))
            f.weights_hi(act)
            over_tiles(act, body)
            finish(Tile(T // 2 - 1, 1))
            for p in range(2):
                act.wait_ge(vo_out[p], 16 * (T // 2))
                act.wait_ge(an_out[p], 16 * (T // 2))

        @block.vector
        def _(dve):
            v = nc.vector

            def layer_norm(tile):
                c = Chain(dve, ln_steps, 7 * tile.t)
                col = lambda n: ln[:, n, :].unsqueeze(2).to_broadcast([P, H, DH])
                flat = lambda x: x[:].rearrange("p h d -> p (h d)")
                dve.wait_ge(vg_ready, tile.t + 1)
                c.then(v.reduce_sum(ln[:, 0, :], vg[:], AX.X))
                c.then(v.tensor_scalar(ln[:, 1, :], ln[:, 0, :], 1.0 / DH, None, ALU.mult))
                c.then(v.tensor_tensor(vc[:], vg[:], col(1), ALU.subtract))
                c.then(v.tensor_tensor(vq[:], vc[:], vc[:], ALU.mult))
                c.then(v.reduce_sum(ln[:, 2, :], vq[:], AX.X))
                inverse_root(nc, Chain(dve, ln_root_steps, ROOT_STEPS * tile.t), 1.0 / DH, ln[:, 2, :],
                             ln_work[:], ln[:, 3, :]).then_inc(ln_rstd_ready, 1)
                dve.wait_ge(ln_rstd_ready, tile.t + 1)
                c.then(v.tensor_tensor(vq[:], vc[:], col(3), ALU.mult))
                c.then(v.tensor_tensor(flat(vc), flat(vq), gains[:], ALU.mult))
                wait(dve, mixed, tile.t)
                v.tensor_tensor(flat(vn), flat(vc), biases[:], ALU.add).then_inc(vn_ready, 1)

            def combine(tile):
                dve.wait_ge(mixed, tile.t + 1)
                wait(dve, a_squares_ready, tile.t)
                dve.wait_ge(ug_ready, tile.t + 1)
                v.tensor_tensor(gt[:], psM[:], bs[:].unsqueeze(2).to_broadcast([P, H, DH]), ALU.add
                                ).then_inc(bias_added, 1)
                dve.wait_ge(bias_added, tile.t + 1)
                wait(dve, an_ready, tile.t)
                v.tensor_tensor(a[:], gt[:], ug[tile.p][:], ALU.mult).then_inc(combined, 1)
                dve.wait_ge(combined, tile.t + 1)
                v.tensor_tensor_reduce(gt[:], a[:], a[:], 1.0, 0.0, ALU.mult, ALU.add, ast[:, 0:1]
                                       ).then_inc(a_squares_ready, 1)
                dve.wait_ge(a_squares_ready, tile.t + 1)
                inverse_root(nc, Chain(dve, a_root_steps, ROOT_STEPS * tile.t), 1.0 / W, ast[:, 0:1],
                             a_work[:], ast[:, 1:2]).then_inc(a_ready, 1)

            def body(tile):
                if tile.has(1):
                    f.lo_x(dve, tile.at(1))
                if tile.has(2):
                    f.rstd(dve, tile.at(2))
                layer_norm(tile)
                if tile.has(-1):
                    combine(tile.at(-1))

            dve.wait_ge(f.g_in, 16)
            f.rstd(dve, Tile(0, 0))
            f.lo_x(dve, Tile(0, 0))
            f.rstd(dve, Tile(0, 1))
            f.weights_lo(dve)
            dve.wait_ge(ws_in, 16)
            dve.wait_ge(tri_in, 16)
            v.tensor_tensor(ws[:], ws[:], tri[:].unsqueeze(1).to_broadcast([P, H, P]), ALU.mult
                            ).then_inc(ws_masked, 1)
            for s in (bs_in, lng_in, lnb_in):
                dve.wait_ge(s, 16)
            over_tiles(dve, body)
            combine(Tile(T // 2 - 1, 1))


def rotary_stage(nc, io, scratch, keep):
    with ExitStack() as ctx:
        sb = lambda s, shape, dt=F32: ctx.enter_context(nc.sbuf_tensor(f"ro_{s}", shape, dt))
        ps = lambda s, shape: ctx.enter_context(nc.psum_tensor(f"ro_ps_{s}", shape, F32))
        sem = stage_semaphores(nc, ctx, "ro")
        f = NormFront(nc, ctx, sem, "ro", keep, io["x"], io["norm1_g"], io["w_in"], (2 * W, 3 * W))
        tab = [sb(f"tab{p}", [P, 2, DH]) for p in range(2)]
        straight, turned_half = sb("straight", [P, H, DH]), sb("turned_half", [P, H, DH])
        rot = [sb(f"rot{n}", [P, H, DH]) for n in range(2)]
        psQ = [ps(f"q{n}", [P, H, DH]) for n in range(2)]
        psR = [ps(f"r{n}", [P, PAIRS, P]) for n in range(2)]
        tab_in = [sem(f"tab_in{p}") for p in range(2)]
        q_done = sem("q_done")
        products = sem("products")
        rot_ready = sem("rot_ready")
        heads_turned = sem("heads_turned")
        heads_kept = sem("heads_kept")
        block = ctx.enter_context(nc.Block())

        @block.sync
        def _(sp):
            def load(tile):
                f.load_x(sp, tile)
                wait(sp, rot_ready, 2 * tile.t - 2)
                sp.dma_start(tab[tile.p][:], io["rope"][tile.rows, :, :]).then_inc(tab_in[tile.p], 16)
            load(Tile(0, 0))
            load(Tile(0, 1))
            f.load_weights(sp)
            with sp.Fori(1, T // 2) as i:
                for p in range(2):
                    load(Tile(i, p))

        @block.gpsimd
        def _(pool):
            def add_halves(tile):
                for n in range(2):
                    pool.wait_ge(products, 2 * tile.t + n + 1)
                    wait(pool, heads_turned, tile.t)
                    nc.gpsimd.tensor_tensor(rot[n][:], straight[:], turned_half[:], ALU.add
                                            ).then_inc(rot_ready, 1)

            over_tiles(pool, add_halves)

        @block.tensor
        def _(pe):
            def turn_heads(tile):
                pe.wait_ge(rot_ready, 2 * tile.t + 2)
                wait(pe, heads_kept, 2 * tile.t)
                for n in range(2):
                    for pr in range(PAIRS):
                        ins = pe.transpose(psR[n][:, pr, :], rot[n][:, 2 * pr:2 * pr + 2, :].rearrange(
                            "p h d -> p (h d)"), keep["ident"][:])
                ins.then_inc(heads_turned, 1)

            def body(tile):
                if tile.has(1):
                    f.turn_x(pe, tile.at(1))
                pe.wait_ge(f.lo_ready, tile.t + 1)
                for n in range(2):
                    wait(pe, products, 2 * tile.t - 1 + n)
                    ins = f.gemm(pe, tile, n, psQ[n][:].rearrange("p h d -> p (h d)"))
                    ins.then_inc(f.gemm_done if n else q_done, 1)
                if tile.has(-1):
                    turn_heads(tile.at(-1))

            f.turn_x(pe, Tile(0, 0))
            over_tiles(pe, body)
            turn_heads(Tile(T // 2 - 1, 1))

        @block.scalar
        def _(act):
            def keep_heads(tile):
                act.wait_ge(heads_turned, tile.t + 1)
                for n, kept in enumerate((keep["qT"], keep["kT"])):
                    nc.scalar.copy(kept[:, :, tile.rows], psR[n][:]).then_inc(heads_kept, 1)

            def body(tile):
                if tile.has(1):
                    f.hi_x(act, tile.at(1))
                if tile.has(2):
                    f.scale_x(act, tile.at(2))
                if tile.has(-1):
                    keep_heads(tile.at(-1))

            act.wait_ge(f.g_in, 16)
            f.scale_x(act, Tile(0, 0))
            f.hi_x(act, Tile(0, 0))
            f.scale_x(act, Tile(0, 1))
            f.weights_hi(act)
            over_tiles(act, body)
            keep_heads(Tile(T // 2 - 1, 1))

        @block.vector
        def _(dve):
            v, half = nc.vector, DH // 2

            def rotate(tile):
                p = tile.p
                dve.wait_ge(tab_in[p], 16 * tile.i + 16)
                table = lambda n, lo, hi: tab[p][:, n, lo:hi].unsqueeze(1).to_broadcast([P, H, hi - lo])
                for n in range(2):
                    if n:
                        dve.wait_ge(f.gemm_done, tile.t + 1)
                    else:
                        dve.wait_ge(q_done, tile.t + 1)
                    wait(dve, rot_ready, 2 * tile.t + n)
                    v.tensor_tensor(straight[:], psQ[n][:], table(0, 0, DH), ALU.mult)
                    v.tensor_tensor(turned_half[:, :, 0:half], psQ[n][:, :, half:DH], table(1, 0, half), ALU.mult)
                    v.tensor_tensor(turned_half[:, :, half:DH], psQ[n][:, :, 0:half], table(1, half, DH), ALU.mult
                                    ).then_inc(products, 1)

            def body(tile):
                if tile.has(1):
                    f.lo_x(dve, tile.at(1))
                if tile.has(2):
                    f.rstd(dve, tile.at(2))
                rotate(tile)

            dve.wait_ge(f.g_in, 16)
            f.rstd(dve, Tile(0, 0))
            f.lo_x(dve, Tile(0, 0))
            f.rstd(dve, Tile(0, 1))
            f.weights_lo(dve)
            over_tiles(dve, body)


class AttentionBlock:

    def __init__(self, branch, g, j):
        self.branch, self.g, self.j = branch, g, j
        self.dil = DILATIONS[branch]
        self.b = 4 * g + j
        self.n = 16 * branch + self.b
        if branch == 0:
            start = self.b * P
            self.has_prev = not (isinstance(g, int) and g == 0 and j == 0)
        elif branch == 1:
            start = g + j * P * self.dil
            self.has_prev = j > 0
        else:
            start = self.b
            self.has_prev = False
        self.tokens = bass.ds(start, P, self.dil)
        self.c0 = 0 if self.has_prev else 1


def over_groups(eng, body):
    body([AttentionBlock(0, 0, j) for j in range(4)])
    with eng.Fori(1, 4) as g:
        body([AttentionBlock(0, g, j) for j in range(4)])
    for branch in (1, 2):
        with eng.Fori(0, 4) as g:
            body([AttentionBlock(branch, g, j) for j in range(4)])


def attention_stage(nc, io, scratch, keep):
    with ExitStack() as ctx:
        sb = lambda s, shape, dt=F32: ctx.enter_context(nc.sbuf_tensor(f"at_{s}", shape, dt))
        ps = lambda s, shape: ctx.enter_context(nc.psum_tensor(f"at_ps_{s}", shape, F32))
        sem = stage_semaphores(nc, ctx, "at")
        qb = [sb(f"q{r}", [P, PAIRS, P]) for r in range(2)]
        kb = [sb(f"k{r}", [P, PAIRS, P]) for r in range(4)]
        vb = [sb(f"v{r}", [P, W]) for r in range(4)]
        mask_in_f32, identb, mask = sb("mask_f32", [P, 2 * P]), sb("identb", [P, P], BF16), sb("mask", [P, 2 * P], BF16)
        prob = [sb(f"p{u}", [P, 2, 2, 2 * P]) for u in range(2)]
        probT = [sb(f"pT{u}", [P, 2, 2, 2, P]) for u in range(2)]
        top = [sb(f"top{u}", [P, 2, 2]) for u in range(2)]
        ob = [sb(f"o{r}", [P, OROW]) for r in range(4)]
        psS = [ps(f"s{u}", [P, 2, 2, 2 * P]) for u in range(2)]
        psT = ps("t", [P, 2, 2, 2, P])
        psO = [ps(f"o{r}", [P, W]) for r in range(2)]

        mask_in, mask_ready = sem("mask_in"), sem("mask_ready")
        v_in = [sem(f"v_in{r}") for r in range(4)]
        blocks_copied = sem("blocks_copied")
        scores_ready, top_ready, negmax_ready = sem("scores_ready"), sem("top_ready"), sem("negmax_ready")
        exp_done, probs_turned = sem("exp_done"), sem("probs_turned")
        kept_by_dve, kept_by_act = sem("kept_by_dve"), sem("kept_by_act")
        weighted = sem("weighted")
        o_ready = sem("o_ready")
        o_out = [sem(f"o_out{r}") for r in range(4)]
        block = ctx.enter_context(nc.Block())

        def units(group):
            return [(blk, u, 2 * blk.n + u) for blk in group for u in range(2)]

        def round_of(blk):
            return 4 * blk.branch + blk.g

        def head(u, half, pr):
            return 2 * (2 * u + pr) + half

        @block.sync
        def _(sp):
            sp.dma_start(mask_in_f32[:], io["band"]).then_inc(mask_in, 16)

            def body(group):
                for blk in group:
                    first = isinstance(blk.n, int) and blk.n < 4
                    if not first:
                        sp.wait_ge(weighted, 2 * blk.n - 4)
                    sp.dma_start(vb[blk.j][:], scratch["v"][blk.tokens, :]).then_inc(v_in[blk.j], 16)
            over_groups(sp, body)

        @block.gpsimd
        def _(pool):
            def body(group):
                for blk in group:
                    if not (isinstance(blk.n, int) and blk.n < 2):
                        pool.wait_ge(scores_ready, 2 * blk.n - 2)
                    nc.gpsimd.tensor_copy(qb[blk.j % 2][:], keep["qT"][:, :, blk.tokens]).then_inc(blocks_copied, 1)
                    nc.gpsimd.tensor_copy(kb[blk.j][:], keep["kT"][:, :, blk.tokens]).then_inc(blocks_copied, 1)
            over_groups(pool, body)

        @block.tensor
        def _(pe):
            def scores(blk, u, n):
                pe.wait_ge(blocks_copied, 2 * blk.n + 2)
                wait(pe, exp_done, n - 1)
                cols = slice(blk.c0 * P, 2 * P)
                for half in range(2):
                    part = slice(DH * half, DH * half + DH)
                    for pr in range(2):
                        pe.matmul(psS[u][:, half, pr, cols], identb[:], mask[:, cols], start=True, stop=False)
                        for c in range(blk.c0, 2):
                            ins = pe.matmul(psS[u][:, half, pr, c * P:(c + 1) * P],
                                            qb[blk.j % 2][part, 2 * u + pr, :],
                                            kb[(blk.j - 1 + c) % 4][part, 2 * u + pr, :],
                                            start=False, stop=(c == 1))
                ins.then_inc(scores_ready, 1)

            def turn(blk, u, n):
                pe.wait_ge(exp_done, n + 1)
                wait(pe, kept_by_dve, n)
                wait(pe, kept_by_act, n)
                for half in range(2):
                    for pr in range(2):
                        for c in range(blk.c0, 2):
                            ins = pe.transpose(psT[:, half, pr, c, :], prob[u][:, half, pr, c * P:(c + 1) * P],
                                               keep["ident"][:])
                ins.then_inc(probs_turned, 1)

            def weigh(blk, u, n):
                pe.wait_ge(kept_by_dve, n + 1)
                pe.wait_ge(kept_by_act, n + 1)
                if u == 0:
                    wait(pe, o_ready, blk.n - 1)
                    pe.wait_ge(v_in[blk.j], 16 * round_of(blk) + 16)
                for half in range(2):
                    for pr in range(2):
                        cols = slice(DH * head(u, half, pr), DH * head(u, half, pr) + DH)
                        for c in range(blk.c0, 2):
                            ins = pe.matmul(psO[blk.j % 2][:, cols], probT[u][:, half, pr, c, :],
                                            vb[(blk.j - 1 + c) % 4][:, cols], start=(c == blk.c0), stop=(c == 1))
                ins.then_inc(weighted, 1)

            def body(group):
                us = units(group)
                for s in range(len(us) + 2):
                    if s < len(us):
                        scores(*us[s])
                    if 1 <= s <= len(us):
                        turn(*us[s - 1])
                    if s >= 2:
                        weigh(*us[s - 2])
            pe.wait_ge(mask_ready, 2)
            over_groups(pe, body)

        @block.scalar
        def _(act):
            def exponentials(blk, u, n):
                act.wait_ge(negmax_ready, n + 1)
                wait(act, probs_turned, n - 1)
                for half in range(2):
                    for pr in range(2):
                        h = head(u, half, pr)
                        ins = nc.scalar.activation(
                            prob[u][:, half, pr, blk.c0 * P:2 * P], psS[u][:, half, pr, blk.c0 * P:2 * P], ACT.Exp,
                            bias=ob[blk.j][:, W + h:W + h + 1], scale=SCALE,
                            accum_out=ob[blk.j][:, W + H + h:W + H + h + 1])
                ins.then_inc(exp_done, 1)

            def keep_half(blk, u, n):
                act.wait_ge(probs_turned, n + 1)
                wait(act, weighted, n - 1)
                nc.scalar.copy(probT[u][:, 1, :, blk.c0:2, :], psT[:, 1, :, blk.c0:2, :]).then_inc(kept_by_act, 1)

            def store(blk):
                act.wait_ge(o_ready, blk.n + 1)
                act.wait_ge(exp_done, 2 * blk.n + 2)
                act.dma_start(scratch["o"][blk.branch, blk.tokens, :], ob[blk.j][:]
                              ).then_inc(o_out[blk.j], 16)

            def body(group):
                us = units(group)
                for s in range(len(us) + 3):
                    if s < len(us):
                        exponentials(*us[s])
                    if 1 <= s <= len(us):
                        keep_half(*us[s - 1])
                    if s >= 4 and s % 2 == 0:
                        store(us[s - 4][0])
            over_groups(act, body)
            for r in range(4):
                act.wait_ge(o_out[r], 16 * 3 * T // 4)

        @block.vector
        def _(dve):
            v = nc.vector

            def maxima(blk, u, n):
                dve.wait_ge(scores_ready, n + 1)
                wait(dve, negmax_ready, n - 1)
                v.tensor_reduce(top[u][:], psS[u][:, :, :, blk.c0 * P:2 * P], AX.X, ALU.max).then_inc(top_ready, 1)
                dve.wait_ge(top_ready, n + 1)
                if u == 0:
                    wait(dve, o_out[blk.j], 16 * round_of(blk))
                v.tensor_scalar(ob[blk.j][:, W + 4 * u:W + 4 * u + 4].rearrange("p (a b) -> p b a", b=2),
                                top[u][:], -SCALE, None, ALU.mult).then_inc(negmax_ready, 1)

            def keep_half(blk, u, n):
                dve.wait_ge(probs_turned, n + 1)
                wait(dve, weighted, n - 1)
                v.tensor_copy(probT[u][:, 0, :, blk.c0:2, :], psT[:, 0, :, blk.c0:2, :]).then_inc(kept_by_dve, 1)

            def outputs(blk):
                dve.wait_ge(weighted, 2 * blk.n + 2)
                v.tensor_copy(ob[blk.j][:, 0:W], psO[blk.j % 2][:]).then_inc(o_ready, 1)

            def body(group):
                us = units(group)
                for s in range(len(us) + 2):
                    if s < len(us):
                        maxima(*us[s])
                    if 1 <= s <= len(us):
                        keep_half(*us[s - 1])
                    if s >= 3 and s % 2 == 1:
                        outputs(us[s - 2][0])

            dve.wait_ge(mask_in, 16)
            v.tensor_copy(identb[:], keep["ident"][:]).then_inc(mask_ready, 1)
            v.tensor_copy(mask[:], mask_in_f32[:]).then_inc(mask_ready, 1)
            over_groups(dve, body)


def mixing_stage(nc, io, scratch, keep):
    with ExitStack() as ctx:
        sb = lambda s, shape, dt=F32: ctx.enter_context(nc.sbuf_tensor(f"mi_{s}", shape, dt))
        ps = lambda s, shape: ctx.enter_context(nc.psum_tensor(f"mi_ps_{s}", shape, F32))
        sem = stage_semaphores(nc, ctx, "mi")
        NB = len(DILATIONS)
        mixed = [sb(f"mixed{p}", [P, D]) for p in range(2)]
        f = Front(nc, ctx, sem, "mi", keep, io["mix_g"], io["w_out"], (0, W), rows=mixed)
        rows_o = [sb(f"rows{p}", [P, NB, OROW]) for p in range(2)]
        xt = [sb(f"x{p}", [P, D]) for p in range(2)]
        low, total, inverse = sb("low", [P, H]), sb("total", [P, H]), sb("inverse", [P, H])
        diff, weight, share = sb("diff", [P, NB, H]), sb("weight", [P, NB, H]), sb("share", [P, NB, H])
        coef = [sb(f"coef{p}", [P, NB, H]) for p in range(2)]
        scaled = sb("scaled", [P, NB, H, DH])
        partial = sb("partial", [P, H, DH])
        bo = [sb(f"bo{p}", [P, H, DH]) for p in range(2)]
        squares = sb("squares", [P, D])
        bst, hst = sb("bst", [P, 2, 2]), sb("hst", [P, 2, 2])
        work = sb("work", [P, ROOT_WORK, 1])
        h = [sb(f"h{p}", [P, D]) for p in range(2)]
        hs = [sb(f"hs{p}", [P, D]) for p in range(2)]
        hT = sb("hT", [P, KD, P])
        g2, wr, br = sb("g2", [P, KD]), sb("wr", [P, KD, E]), sb("br", [P, E])
        psH = [ps(f"h{n}", [P, W]) for n in range(2)]
        psT = ps("hT", [P, KD, P])
        psR = ps("r", [P, E])

        o_in, a_in, x_in, h_out, hs_out = ([sem(f"{s}{p}") for p in range(2)]
                                           for s in ("o_in", "a_in", "x_in", "h_out", "hs_out"))
        g2_in, wr_in, br_in = sem("g2_in"), sem("wr_in"), sem("br_in")
        low_ready, diff_ready, weight_ready = sem("low_ready"), sem("diff_ready"), sem("weight_ready")
        coef_steps, coef_ready = sem("coef_steps"), sem("coef_ready")
        scaled_ready, partial_ready, bo_ready = sem("scaled_ready"), sem("partial_ready"), sem("bo_ready")
        b_squares, b_root, b_scale = sem("b_squares"), sem("b_root"), sem("b_scale")
        half_done = sem("half_done")
        h_halves, h_squares, h_root, h_scale = sem("h_halves"), sem("h_squares"), sem("h_root"), sem("h_scale")
        hs_ready, h_turned, hT_ready, routed = sem("hs_ready"), sem("h_turned"), sem("hT_ready"), sem("routed")
        logits_ready = sem("logits_ready")
        block = ctx.enter_context(nc.Block())

        @block.sync
        def _(sp):
            def load(tile):
                p = tile.p
                wait(sp, scaled_ready, tile.t - 1)
                sp.dma_start(rows_o[p][:], scratch["o"][:, tile.rows, :].rearrange("b p w -> p b w")
                             ).then_inc(o_in[p], 16)
                wait(sp, f.turned, tile.t - 1)
                sp.dma_start(mixed[p][:, 0:W], scratch["a"][tile.rows, :]).then_inc(a_in[p], 16)

            def load_x(tile):
                wait(sp, h_halves, 2 * tile.t - 2)
                sp.dma_start(xt[tile.p][:], io["x"][tile.rows, :]).then_inc(x_in[tile.p], 16)

            load(Tile(0, 0))
            load(Tile(0, 1))
            f.load_weights(sp)
            sp.dma_start(g2[:], io["norm2_g"]).then_inc(g2_in, 16)
            sp.dma_start(wr[:], io["w_router"]).then_inc(wr_in, 16)
            sp.dma_start(br[:], io["b_router"].to_broadcast([P, E])).then_inc(br_in, 16)
            load_x(Tile(0, 0))
            with sp.Fori(1, T // 2) as i:
                for p in range(2):
                    load(Tile(i, p))
                    load_x(Tile(i, p).at(-1))
            load_x(Tile(T // 2 - 1, 1))

        @block.gpsimd
        def _(pool):
            def sum_branches(tile):
                p, t, g = tile.p, tile.t, nc.gpsimd
                pool.wait_ge(coef_ready, t + 1)
                wait(pool, bo_ready, t)
                g.tensor_tensor(scaled[:], rows_o[p][:, :, 0:W].rearrange("p b (h d) -> p b h d", h=H),
                                coef[p][:].unsqueeze(3).to_broadcast([P, NB, H, DH]), ALU.mult
                                ).then_inc(scaled_ready, 1)
                pool.wait_ge(scaled_ready, t + 1)
                g.tensor_tensor(partial[:], scaled[:, 0], scaled[:, 1], ALU.add).then_inc(partial_ready, 1)
                pool.wait_ge(partial_ready, t + 1)
                wait(pool, f.xn_ready, t - 1)
                g.tensor_tensor(bo[p][:], partial[:], scaled[:, 2], ALU.add).then_inc(bo_ready, 1)
            over_tiles(pool, sum_branches)

        @block.tensor
        def _(pe):
            def turn_mixed(tile):
                pe.wait_ge(a_in[tile.p], 16 * tile.i + 16)
                f.turn_x(pe, tile)

            def turn_hidden(tile):
                pe.wait_ge(hs_ready, tile.t + 1)
                wait(pe, hT_ready, tile.t)
                for k in range(KD):
                    ins = pe.transpose(psT[:, k, :], hs[tile.p][:, k * P:(k + 1) * P], keep["ident"][:])
                ins.then_inc(h_turned, 1)

            def route(tile):
                pe.wait_ge(hT_ready, tile.t + 1)
                wait(pe, logits_ready, tile.t)
                for k in range(KD):
                    ins = pe.matmul(psR[:], hT[:, k, :], wr[:, k, :], start=(k == 0), stop=(k == KD - 1))
                ins.then_inc(routed, 1)

            def body(tile):
                if tile.has(1):
                    turn_mixed(tile.at(1))
                pe.wait_ge(f.lo_ready, tile.t + 1)
                for n in range(2):
                    wait(pe, h_halves, 2 * tile.t + n - 1)
                    ins = f.gemm(pe, tile, n, psH[n][:])
                    ins.then_inc(f.gemm_done if n else half_done, 1)
                if tile.has(-2):
                    route(tile.at(-2))
                if tile.has(-1):
                    turn_hidden(tile.at(-1))

            turn_mixed(Tile(0, 0))
            pe.wait_ge(wr_in, 16)
            over_tiles(pe, body, 3)
            route(Tile(T // 2 - 1, 0))
            turn_hidden(Tile(T // 2 - 1, 1))
            route(Tile(T // 2 - 1, 1))

        @block.scalar
        def _(act):
            def weights(tile):
                act.wait_ge(diff_ready, tile.t + 1)
                wait(act, coef_ready, tile.t)
                nc.scalar.activation(weight[:], diff[:], ACT.Exp).then_inc(weight_ready, 1)

            def scale_b(tile):
                act.wait_ge(b_scale, tile.t + 1)
                wait(act, f.turned, tile.t - 1)
                nc.scalar.mul(mixed[tile.p][:, W:D], bo[tile.p][:].rearrange("p h d -> p (h d)"),
                              bst[:, tile.p, 1:2]).then_inc(f.xn_ready, 1)

            def scale_hidden(tile):
                p = tile.p
                act.wait_ge(h_scale, tile.t + 1)
                wait(act, hs_out[p], 16 * tile.i)
                wait(act, h_turned, tile.t - 1)
                nc.scalar.mul(hs[p][:], h[p][:], hst[:, p, 1:2]).then_inc(hs_ready, 1)
                act.dma_start(scratch["h"][tile.rows, :], h[p][:]).then_inc(h_out[p], 16)
                act.wait_ge(hs_ready, tile.t + 1)
                act.dma_start(scratch["hn"][tile.rows, :], hs[p][:]).then_inc(hs_out[p], 16)

            def keep_hidden(tile):
                act.wait_ge(h_turned, tile.t + 1)
                wait(act, routed, tile.t)
                for k in range(KD):
                    ins = nc.scalar.mul(hT[:, k, :], psT[:, k, :], g2[:, k:k + 1])
                ins.then_inc(hT_ready, 1)

            def body(tile):
                if tile.has(1):
                    f.hi_x(act, tile.at(1))
                if tile.has(3):
                    weights(tile.at(3))
                if tile.has(-1):
                    scale_hidden(tile.at(-1))
                if tile.has(2):
                    scale_b(tile.at(2))
                if tile.has(-1):
                    keep_hidden(tile.at(-1))

            act.wait_ge(f.g_in, 16)
            act.wait_ge(g2_in, 16)
            weights(Tile(0, 0))
            weights(Tile(0, 1))
            scale_b(Tile(0, 0))
            f.hi_x(act, Tile(0, 0))
            scale_b(Tile(0, 1))
            weights(Tile(1, 0))
            f.weights_hi(act)
            over_tiles(act, body, 3)
            scale_hidden(Tile(T // 2 - 1, 1))
            keep_hidden(Tile(T // 2 - 1, 1))
            for p in range(2):
                act.wait_ge(h_out[p], 16 * (T // 2))
                act.wait_ge(hs_out[p], 16 * (T // 2))

        @block.vector
        def _(dve):
            v = nc.vector

            def distances(tile):
                p, t = tile.p, tile.t
                negmax = rows_o[p][:, :, W:W + H]
                dve.wait_ge(o_in[p], 16 * tile.i + 16)
                wait(dve, diff_ready, t)
                v.tensor_reduce(low[:], negmax.rearrange("p b h -> p h b"), AX.X, ALU.min).then_inc(low_ready, 1)
                dve.wait_ge(low_ready, t + 1)
                wait(dve, weight_ready, t)
                v.tensor_tensor(diff[:], low[:].unsqueeze(1).to_broadcast([P, NB, H]), negmax, ALU.subtract
                                ).then_inc(diff_ready, 1)

            def coefficients(tile):
                p, t = tile.p, tile.t
                c = Chain(dve, coef_steps, 3 * t)
                dve.wait_ge(weight_ready, t + 1)
                c.then(v.tensor_tensor(share[:], weight[:], rows_o[p][:, :, W + H:OROW], ALU.mult))
                c.then(v.reduce_sum(total[:], share[:].rearrange("p b h -> p h b"), AX.X))
                c.then(v.reciprocal(inverse[:], total[:]))
                wait(dve, scaled_ready, t - 1)
                v.tensor_tensor(coef[p][:], weight[:], inverse[:].unsqueeze(1).to_broadcast([P, NB, H]), ALU.mult
                                ).then_inc(coef_ready, 1)

            def norm_b(tile):
                p, t = tile.p, tile.t
                flat = bo[p][:].rearrange("p h d -> p (h d)")
                dve.wait_ge(bo_ready, t + 1)
                wait(dve, f.xn_ready, t - 1)
                v.tensor_tensor_reduce(squares[:, 0:W], flat, flat, 1.0, 0.0, ALU.mult, ALU.add, bst[:, p, 0:1]
                                       ).then_inc(b_squares, 1)
                dve.wait_ge(b_squares, t + 1)
                inverse_root(nc, Chain(dve, b_root, ROOT_STEPS * t), 1.0 / W, bst[:, p, 0:1], work[:],
                             bst[:, p, 1:2]).then_inc(b_scale, 1)
                dve.wait_ge(b_scale, t + 1)

            def residual(tile):
                p, t = tile.p, tile.t
                dve.wait_ge(x_in[p], 16 * tile.i + 16)
                wait(dve, h_out[p], 16 * tile.i)
                for n in range(2):
                    if n:
                        dve.wait_ge(f.gemm_done, t + 1)
                    else:
                        dve.wait_ge(half_done, t + 1)
                    cols = slice(n * W, n * W + W)
                    v.tensor_tensor(h[p][:, cols], psH[n][:], xt[p][:, cols], ALU.add).then_inc(h_halves, 1)
                dve.wait_ge(h_halves, 2 * t + 2)
                v.tensor_tensor_reduce(squares[:], h[p][:], h[p][:], 1.0, 0.0, ALU.mult, ALU.add, hst[:, p, 0:1]
                                       ).then_inc(h_squares, 1)
                dve.wait_ge(h_squares, t + 1)
                inverse_root(nc, Chain(dve, h_root, ROOT_STEPS * t), 1.0 / D, hst[:, p, 0:1], work[:],
                             hst[:, p, 1:2]).then_inc(h_scale, 1)
                dve.wait_ge(h_scale, t + 1)

            def keep_logits(tile):
                dve.wait_ge(routed, tile.t + 1)
                v.tensor_tensor(keep["logits"][:, bass.ds(tile.t, 1), :], psR[:].unsqueeze(1),
                                br[:].unsqueeze(1), ALU.add).then_inc(logits_ready, 1)

            def body(tile):
                if tile.has(1):
                    f.lo_x(dve, tile.at(1))
                if tile.has(3):
                    distances(tile.at(3))
                if tile.has(2):
                    norm_b(tile.at(2))
                if tile.has(3):
                    coefficients(tile.at(3))
                residual(tile)
                if tile.has(-2):
                    keep_logits(tile.at(-2))

            dve.wait_ge(f.g_in, 16)
            for tile in (Tile(0, 0), Tile(0, 1)):
                distances(tile)
                coefficients(tile)
            norm_b(Tile(0, 0))
            f.lo_x(dve, Tile(0, 0))
            norm_b(Tile(0, 1))
            distances(Tile(1, 0))
            coefficients(Tile(1, 0))
            f.weights_lo(dve)
            dve.wait_ge(br_in, 16)
            over_tiles(dve, body, 3)
            keep_logits(Tile(T // 2 - 1, 0))
            keep_logits(Tile(T // 2 - 1, 1))


PE_WIDTHS = (192, 256, 320, 384, SLOT)
TILE_WIDTHS = (256, 384, SLOT)
EXPERT, PE_CLASS, TILE_CLASS, USED = range(4)
ENTRY = 4


def routing_stage(nc, io, scratch, keep):
    with ExitStack() as ctx:
        sb = lambda s, shape, dt=F32: ctx.enter_context(nc.sbuf_tensor(f"rt_{s}", shape, dt))
        sem = stage_semaphores(nc, ctx, "rt")
        blank = sb("blank", [P, LIST_ROWS // P, LROW], U32)
        token = sb("token", [P, T])
        token_rows = sb("token_rows", [P, T, TOPK, LROW], U32)
        expert, slot, before, ones = sb("expert", [P, E]), sb("slot", [P, 1]), sb("before", [P, P]), sb("ones", [P, P])
        topv, topi, chosen = sb("topv", [P, T, 8]), sb("topi", [P, T, 8], U32), sb("chosen", [P, T, TOPK])
        shifted, power, power_sum = sb("shifted", [P, T, TOPK]), sb("power", [P, T, TOPK]), sb("power_sum", [P, T])
        power_inv = sb("power_inv", [P, T])
        hot = sb("hot", [P, TOPK, T, E])
        picked = sb("picked", [P, T, E])
        weighted = sb("weighted", [P, T, E])
        tile_counts, running = sb("tile_counts", [P, E, T]), sb("running", [P, E, T])
        restart = sb("restart", [P, E, T])
        slots_of, slot_end, slot_first = sb("slots_of", [P, E]), sb("slot_end", [P, E]), sb("slot_first", [P, E])
        row_first, row_end = sb("row_first", [P, E]), sb("row_end", [P, E])
        position = sb("position", [P, T, E])
        places = sb("places", [P, T, TOPK])
        ended, begun, left = sb("ended", [P, E]), sb("begun", [P, E]), sb("left", [P, E])
        tokens_of, entry, entry_i = sb("tokens_of", [P, 2]), sb("entry", [P, ENTRY]), sb("entry_i", [P, ENTRY], I32)
        slot_rows = sb("slot_rows", [P, 1])
        psRank = ctx.enter_context(nc.psum_tensor("rt_ps_rank", [P, T, E], F32))
        psCount = ctx.enter_context(nc.psum_tensor("rt_ps_count", [P, T, E], F32))

        consts_in = [sem(f"in_{n}") for n in range(4)]
        listed, blank_ready = sem("listed"), sem("blank_ready")
        steps = sem("steps")
        max_ready, exp_ready, picked_ready, ranked = sem("max_ready"), sem("exp_ready"), sem("picked_ready"), sem("ranked")
        places_ready, table_ready, tokens_ready = sem("places_ready"), sem("table_ready"), sem("tokens_ready")
        scattered, table_out, table_back = sem("scattered"), sem("table_out"), sem("table_back")
        block = ctx.enter_context(nc.Block())

        @block.sync
        def _(sp):
            for n, (dst, src) in enumerate(((token[:], io["token"]), (expert[:], io["expert"].to_broadcast([P, E])),
                                            (slot[:], io["slot"]), (before[:], io["before"]))):
                sp.dma_start(dst, src).then_inc(consts_in[n], 16)
            sp.wait_ge(blank_ready, 3)
            sp.dma_start(scratch["list"].rearrange("(p r) w -> p (r w)", p=P),
                         blank[:].rearrange("p r w -> p (r w)")).then_inc(listed, 16)
            sp.wait_ge(table_ready, 1)
            sp.dma_start(scratch["table"], entry_i[0:NSLOTS + 1, :]).then_inc(table_out, 16)
            sp.wait_ge(table_out, 16)
            sp.dma_start(keep["table"][:], scratch["table"].rearrange("s w -> (s w)").rearrange("(a n) -> a n", a=1)
                         ).then_inc(table_back, 16)
            sp.wait_ge(table_back, 16)

        @block.gpsimd
        def _(pool):
            nc.gpsimd.memset(blank[:], 0).then_inc(blank_ready, 1)
            pool.wait_ge(blank_ready, 1)
            for half in range(2):
                nc.gpsimd.iota(blank[:, :, 1 + half], pattern=[[2, LIST_ROWS // P]], base=2 * S * TOPK + half,
                               channel_multiplier=2 * LIST_ROWS // P).then_inc(blank_ready, 1)
            pool.wait_ge(tokens_ready, 1)
            pool.wait_ge(listed, 16)
            pool.wait_ge(places_ready, 1)
            for t in range(T):
                for k in range(TOPK):
                    nc.gpsimd.indirect_dma_start(
                        out=scratch["list"], out_offset=bass.IndirectOffsetOnAxis(ap=keep["posn"][:, t, k:k + 1], axis=0),
                        in_=token_rows[:, t, k, :], in_offset=None).then_inc(scattered, 16)
            pool.wait_ge(scattered, 16 * T * TOPK)

        @block.tensor
        def _(pe):
            pe.wait_ge(consts_in[3], 16)
            pe.wait_ge(picked_ready, 1)
            flat = picked[:].rearrange("p t e -> p (t e)")
            pe.matmul(psCount[:].rearrange("p t e -> p (t e)"), ones[:], flat, start=True, stop=True)
            pe.matmul(psRank[:].rearrange("p t e -> p (t e)"), before[:], flat, start=True, stop=True
                      ).then_inc(ranked, 1)

        @block.scalar
        def _(act):
            act.wait_ge(max_ready, 1)
            nc.scalar.activation(power[:], shifted[:], ACT.Exp).then_inc(exp_ready, 1)

        @block.vector
        def _(dve):
            v = nc.vector
            c = Chain(dve, steps, 0)
            wide = lambda x: x.unsqueeze(1).to_broadcast([P, T, E])
            v.memset(ones[:], 1.0)
            v.memset(restart[:], 1.0)
            v.memset(token_rows[:], 0)
            for t in range(T):
                last = v.max(topv[:, t, :], keep["logits"][:, t, :])
            c.then(last)
            v.memset(restart[:, :, 0:1], 0.0)
            for t in range(T):
                v.max_index(topi[:, t, :], topv[:, t, :], keep["logits"][:, t, :])
            c.then(v.tensor_tensor(shifted[:], topv[:, :, 0:TOPK], topv[:, :, 0:1].to_broadcast([P, T, TOPK]),
                                   ALU.subtract))
            v.tensor_copy(chosen[:], topi[:, :, 0:TOPK]).then_inc(max_ready, 1)
            dve.wait_ge(max_ready, 1)
            dve.wait_ge(consts_in[0], 16)
            for k in range(TOPK):
                v.tensor_copy(token_rows[:, :, k, 0], token[:])
                for half in range(2):
                    last = v.tensor_scalar(token_rows[:, :, k, 1 + half], token[:], 2.0 * TOPK, 2.0 * k + half,
                                           ALU.mult, ALU.add)
            last.then_inc(tokens_ready, 1)
            dve.wait_ge(consts_in[1], 16)
            for k in range(TOPK):
                last = v.tensor_tensor(hot[:, k], wide(expert[:]), chosen[:, :, k:k + 1].to_broadcast([P, T, E]),
                                       ALU.is_equal)
            c.then(last)
            v.tensor_tensor(position[:], hot[:, 0], hot[:, 1], ALU.add)
            c.then(v.tensor_tensor(weighted[:], hot[:, 2], hot[:, 3], ALU.add))
            v.tensor_tensor(picked[:], position[:], weighted[:], ALU.add).then_inc(picked_ready, 1)
            dve.wait_ge(picked_ready, 1)
            dve.wait_ge(exp_ready, 1)
            c.then(v.reduce_sum(power_sum[:], power[:], AX.X))
            c.then(v.reciprocal(power_inv[:], power_sum[:]))
            c.then(v.tensor_tensor(keep["gates"][:], power[:], power_inv[:].unsqueeze(2).to_broadcast([P, T, TOPK]),
                                   ALU.mult))
            c.then(v.tensor_tensor(keep["spread"][:], hot[:, 0], keep["gates"][:, :, 0:1].to_broadcast([P, T, E]),
                                   ALU.mult))
            for k in range(1, TOPK):
                c.then(v.tensor_tensor(weighted[:], hot[:, k], keep["gates"][:, :, k:k + 1].to_broadcast([P, T, E]),
                                       ALU.mult))
                c.then(v.tensor_tensor(keep["spread"][:], keep["spread"][:], weighted[:], ALU.add))
            dve.wait_ge(ranked, 1)
            c.then(v.tensor_copy(tile_counts[:], psCount[:].rearrange("p t e -> p e t")))
            c.then(v.tensor_tensor_scan(running[:].rearrange("p e t -> p (e t)"), restart[:].rearrange("p e t -> p (e t)"),
                                        tile_counts[:].rearrange("p e t -> p (e t)"), 0.0, ALU.mult, ALU.add))
            counts = running[:, :, T - 1]
            c.then(v.tensor_scalar(slots_of[:], counts, 0.0, None, ALU.is_gt))
            for j in range(1, S // SLOT):
                c.then(v.scalar_tensor_tensor(slots_of[:], counts, float(SLOT * j), slots_of[:], ALU.is_gt, ALU.add))
            c.then(v.tensor_tensor_scan(slot_end[:], ones[:, 0:E], slots_of[:], 0.0, ALU.mult, ALU.add))
            c.then(v.tensor_tensor(slot_first[:], slot_end[:], slots_of[:], ALU.subtract))
            c.then(v.tensor_scalar(row_first[:], slot_first[:], float(SLOT), None, ALU.mult))
            c.then(v.tensor_tensor(row_end[:], row_first[:], counts, ALU.add))
            c.then(v.tensor_tensor(running[:], running[:], tile_counts[:], ALU.subtract))
            c.then(v.tensor_tensor(position[:], psRank[:], running[:].rearrange("p e t -> p t e"), ALU.add))
            c.then(v.tensor_tensor(position[:], position[:], wide(row_first[:]), ALU.add))
            for k in range(TOPK):
                c.then(v.tensor_tensor(weighted[:], hot[:, k], position[:], ALU.mult))
                c.then(v.reduce_sum(places[:, :, k], weighted[:], AX.X))
            v.tensor_copy(keep["posn"][:], places[:]).then_inc(places_ready, 1)
            dve.wait_ge(consts_in[2], 16)
            c.then(v.tensor_scalar(slot_rows[:], slot[:], float(SLOT), None, ALU.mult))
            v.tensor_scalar(ended[:], slot_end[:], slot[:, 0:1], None, ALU.is_le)
            v.tensor_scalar(begun[:], slot_first[:], slot[:, 0:1], None, ALU.is_le)
            c.then(v.tensor_scalar(left[:], row_end[:], slot_rows[:, 0:1], None, ALU.subtract))
            c.then(v.tensor_tensor(begun[:], begun[:], ended[:], ALU.subtract))
            c.then(v.tensor_tensor(left[:], left[:], begun[:], ALU.mult))
            v.reduce_sum(tokens_of[:, 0:1], ended[:], AX.X)
            c.then(v.reduce_sum(tokens_of[:, 1:2], left[:], AX.X))
            v.tensor_scalar(entry[:, EXPERT:EXPERT + 1], tokens_of[:, 0:1], float(E - 1), None, ALU.min)
            v.tensor_copy(entry[:, USED:USED + 1], slot_end[:, E - 1:E])
            for column, widths in ((PE_CLASS, PE_WIDTHS), (TILE_CLASS, TILE_WIDTHS)):
                kind = entry[:, column:column + 1]
                c.then(v.tensor_scalar(kind, tokens_of[:, 1:2], 0.0, None, ALU.is_gt))
                for w in widths[:-1]:
                    c.then(v.scalar_tensor_tensor(kind, tokens_of[:, 1:2], float(w), kind, ALU.is_gt, ALU.add))
            v.tensor_copy(entry_i[:], entry[:]).then_inc(table_ready, 1)


def tile_count(width):
    return -(-width // P)


def table_entry(eng, keep, s, column, most):
    return eng.value_load(keep["table"][0:1, bass.ds(ENTRY * s + column, 1)], min_val=0, max_val=most)


def over_slots(eng, keep, column, widths, body):
    with eng.Fori(0, NSLOTS) as s:
        kind = table_entry(eng, keep, s, column, len(widths))
        for c, width in enumerate(widths):
            with eng.If(kind == c + 1):
                body(s, width)


def experts_stage(nc, io, scratch, keep):
    CH = 6
    HALF = 512
    FB = HALF // P
    BANKS = 4
    USES = 3 * KD
    with ExitStack() as ctx:
        sb = lambda s, shape, dt=F32: ctx.enter_context(nc.sbuf_tensor(f"ex_{s}", shape, dt))
        ps = lambda s, shape: ctx.enter_context(nc.psum_tensor(f"ex_ps_{s}", shape, F32))
        sem = stage_semaphores(nc, ctx, "ex")
        raw = [sb(f"raw{r}", [P, KD, HALF]) for r in range(2)]
        w = [sb(f"w{r}", [P, 2, KD, HALF], F32R) for r in range(2)]
        idx, dest = sb("idx", [P, ST, LROW], U32), sb("dest", [P, ST, 2], U32)
        xg = sb("xg", [P, ST, D])
        xT = sb("xT", [P, 2, KD, SLOT], F32R)
        gate = sb("gate", [P, FB, SLOT])
        sig = [sb(f"sig{r}", [P, SLOT]) for r in range(2)]
        up = [sb(f"up{r}", [P, SLOT]) for r in range(2)]
        actT = sb("actT", [P, 2, 2 * FB, SLOT], F32R)
        y = sb("y", [P, ST, HALF])
        bgu, bias, g2 = sb("bgu", [P, E, 2 * FF // P]), sb("bias", [P, 2 * FF // P]), sb("g2", [P, KD])
        ring = [ps(f"ring{b}", [P, SLOT]) for b in range(BANKS)]
        psY = [ps(f"y{j}", [P, HALF]) for j in range(ST)]

        raw_in = [sem(f"raw_in{r}") for r in range(2)]
        bgu_in, g2_in = sem("bgu_in"), sem("g2_in")
        idx_in, x_in = sem("idx_in"), sem("x_in")
        w_hi, w_lo = sem("w_hi"), sem("w_lo")
        banks_zeroed = sem("banks_zeroed")
        bank_full, bank_free = sem("bank_full"), sem("bank_free")
        x_hi = sem("x_hi")
        bias_ready = sem("bias_ready")
        sig_ready, swish_ready = sem("sig_ready"), sem("swish_ready")
        up_ready, act_ready = sem("up_ready"), sem("act_ready")
        act_hi, act_lo = sem("act_hi"), sem("act_lo")
        y_full, y_free = sem("y_full"), sem("y_free")
        y_out = sem("y_out")
        dest_ready = sem("dest_ready")
        gather_go, scatter_go, all_stored = sem("gather_go"), sem("scatter_go"), sem("all_stored")
        block = ctx.enter_context(nc.Block())

        def chunk_done(q_of):
            s, c = q_of
            if c < 4:
                return bank_full, KD + USES * s + 4 * (c + 1)
            return y_full, 2 * ST * s + ST * (c - 3)

        @block.sync
        def _(sp):
            def load(e, c):
                if c < 4:
                    c0 = (c % 2) * FF + (c // 2) * HALF
                    src = io["w_gate_up"][bass.ds(e, 1), :, c0:c0 + HALF]
                else:
                    src = io["w_down"][bass.ds(e, 1), :, (c - 4) * HALF:(c - 3) * HALF]
                sp.dma_start(raw[c % 2][:], src.rearrange("o (k p) n -> p (o k) n", p=P)).then_inc(raw_in[c % 2], 16)

            def fetch_tokens(s):
                sp.dma_start(idx[:], scratch["list"][bass.ds(s * SLOT, SLOT), :].rearrange("(j p) w -> p j w", p=P)
                             ).then_inc(idx_in, 16)

            def body(s):
                e, e_next = (table_entry(sp, keep, s + d, EXPERT, E - 1) for d in range(2))
                for c in range(1, CH + 1):
                    if c == 4:
                        sp.wait_ge(dest_ready, s + 1)
                        fetch_tokens(s + 1)
                    sp.wait_ge(w_lo, 2 * (CH * s + c) - 2)
                    load(e if c < CH else e_next, c % CH)

            fetch_tokens(0)
            load(table_entry(sp, keep, 0, EXPERT, E - 1), 0)
            sp.dma_start(bgu[:], io["b_gate_up"]).then_inc(bgu_in, 16)
            sp.dma_start(g2[:], io["norm2_g"]).then_inc(g2_in, 16)
            with sp.Fori(0, NSLOTS) as s:
                with sp.If(table_entry(sp, keep, s, PE_CLASS, len(PE_WIDTHS)) > 0):
                    body(s)

        @block.gpsimd
        def _(pool):
            def gather(s):
                pool.wait_ge(idx_in, 16 * s + 16)
                pool.sem_inc(gather_go, 1)
                for j in range(ST):
                    nc.gpsimd.indirect_dma_start(
                        out=xg[:, j, :], out_offset=None, in_=scratch["hn"],
                        in_offset=bass.IndirectOffsetOnAxis(ap=idx[:, j, 0:1], axis=0)).then_inc(x_in, 16)

            def scatter(s, half, tiles):
                pool.wait_ge(y_free, 2 * ST * s + ST * half + ST)
                pool.sem_inc(scatter_go, 1)
                for j in range(tiles):
                    nc.gpsimd.indirect_dma_start(
                        out=scratch["y"].rearrange("r (h c) -> (r h) c", h=2),
                        out_offset=bass.IndirectOffsetOnAxis(ap=dest[:, j, half:half + 1], axis=0),
                        in_=y[:, j, :], in_offset=None).then_inc(y_out, 16 if j < tiles - 1 else 16 * (ST - tiles + 1))

            def body(s, width):
                g = nc.gpsimd
                for half in range(2):
                    for fb in range(FB):
                        n = 2 * FB * s + FB * half + fb
                        pool.wait_ge(sig_ready, n + 1)
                        g.tensor_tensor(gate[:, fb, 0:width], gate[:, fb, 0:width], sig[fb % 2][:, 0:width], ALU.mult
                                        ).then_inc(swish_ready, 1)
                    for fb in range(FB):
                        n = 2 * FB * s + FB * half + fb
                        pool.wait_ge(swish_ready, n + 1)
                        pool.wait_ge(up_ready, n + 1)
                        g.tensor_tensor(up[fb % 2][:, 0:width], gate[:, fb, 0:width], up[fb % 2][:, 0:width], ALU.mult
                                        ).then_inc(act_ready, 1)
                gather(s + 1)
                for half in range(2):
                    scatter(s, half, tile_count(width))
            gather(0)
            over_slots(pool, keep, TILE_CLASS, TILE_WIDTHS, body)

        @block.tensor
        def _(pe):
            def turn(s, base):
                pe.wait_ge(x_in, 16 * ST * s + 16 * ST)
                for k in range(KD):
                    wait(pe, bank_free, base + k + 1 - BANKS)
                    for j in range(ST):
                        ins = pe.transpose(ring[k % BANKS][:, j * P:(j + 1) * P], xg[:, j, k * P:(k + 1) * P],
                                           keep["ident"][:])
                    ins.then_inc(bank_full, 1)

            def gate_up(s, width):
                with pe.Fori(0, 2) as half:
                    pe.wait_ge(bank_free, KD + USES * s)
                    for up_part in range(2):
                        q = CH * s + 2 * half + up_part
                        pe.wait_ge(w_lo, 2 * q + 2)
                        for fb in range(FB):
                            use = KD + USES * s + 2 * FB * half + FB * up_part + fb
                            pe.wait_ge(bank_free, use + 1 - BANKS)
                            m = 0
                            for k in range(KD):
                                for a, b in SPLIT3:
                                    ins = pe.matmul(ring[fb][:, 0:width], w[up_part][:, a, k, fb * P:(fb + 1) * P],
                                                    xT[:, b, k, 0:width], start=(m == 0), stop=(m == 3 * KD - 1))
                                    m += 1
                            ins.then_inc(bank_full, 1)

            def down(s, width):
                tiles = tile_count(width)
                pe.wait_ge(act_lo, 2 * FB * s + 2 * FB)
                for dh in range(2):
                    pe.wait_ge(w_lo, 2 * (CH * s + 4 + dh) + 2)
                    for j in range(tiles):
                        pe.wait_ge(y_free, 2 * ST * s + (j + 1 if dh else 0))
                        m = 0
                        for f in range(2 * FB):
                            for a, b in SPLIT3:
                                ins = pe.matmul(psY[j][:], actT[:, a, f, j * P:(j + 1) * P], w[dh][:, b, f, :],
                                                start=(m == 0), stop=(m == 6 * FB - 1))
                                m += 1
                        ins.then_inc(y_full, 1 if j < tiles - 1 else ST - tiles + 1)

            def body(s, width):
                gate_up(s, width)
                turn(s + 1, KD + USES * s + 2 * KD)
                down(s, width)

            pe.wait_ge(banks_zeroed, 1)
            turn(0, 0)
            over_slots(pe, keep, PE_CLASS, PE_WIDTHS, body)

        @block.scalar
        def _(act):
            def split_hi(s, c):
                r = c % 2
                act.wait_ge(raw_in[r], 16 * (CH // 2) * s + 16 * (c // 2) + 16)
                if c >= 2:
                    act.wait_ge(*chunk_done((s, c - 2)))
                elif c == 1:
                    act.wait_ge(y_full, 2 * ST * s)
                for part in range(2):
                    ks = slice(part * KD // 2, (part + 1) * KD // 2)
                    nc.scalar.copy(w[r][:, 0, ks, :], raw[r][:, ks, :]).then_inc(w_hi, 1)

            def x_high(s):
                for k in range(KD):
                    act.wait_ge(bank_full, USES * s + k + 1)
                    nc.scalar.mul(xT[:, 0, k, :], ring[k % BANKS][:], g2[:, k:k + 1]).then_inc(x_hi, 1)

            def body(s, width):
                tiles = tile_count(width)
                for c in range(CH):
                    split_hi(s, c + 1)
                    for fb in range(FB if c < 4 else 0):
                        n = 2 * FB * s + FB * (c // 2) + fb
                        if c % 2 == 0:
                            act.wait_ge(bank_free, KD + USES * s + FB * c + fb + 1)
                            act.wait_ge(swish_ready, 2 * FB * s if c == 0 and fb < 2 else n - 1)
                            nc.scalar.activation(sig[fb % 2][:, 0:width], gate[:, fb, 0:width], ACT.Sigmoid,
                                                 scale=ALPHA).then_inc(sig_ready, 1)
                        else:
                            act.wait_ge(act_ready, n + 1)
                            if c == 1 and fb == 0:
                                act.wait_ge(y_full, 2 * ST * s)
                            nc.scalar.copy(actT[:, 0, FB * (c // 2) + fb, 0:width], up[fb % 2][:, 0:width]
                                           ).then_inc(act_hi, 1)
                    if c == 3:
                        x_high(s + 1)
                    if c >= 4:
                        act.wait_ge(y_out, 16 * ST * (2 * s + c - 4))
                        for j in range(tiles):
                            act.wait_ge(y_full, 2 * ST * s + ST * (c - 4) + j + 1)
                            nc.scalar.copy(y[:, j, :], psY[j][:]
                                           ).then_inc(y_free, 1 if j < tiles - 1 else ST - tiles + 1)

            act.wait_ge(g2_in, 16)
            x_high(0)
            split_hi(0, 0)
            over_slots(act, keep, TILE_CLASS, TILE_WIDTHS, body)
            act.wait_ge(y_out, 32 * ST * table_entry(act, keep, 0, USED, NSLOTS))
            act.sem_inc(all_stored, 1)

        @block.vector
        def _(dve):
            v = nc.vector

            def split_lo(s, c):
                r = c % 2
                for part in range(2):
                    ks = slice(part * KD // 2, (part + 1) * KD // 2)
                    dve.wait_ge(w_hi, 2 * (CH * s + c) + part + 1)
                    v.tensor_tensor(w[r][:, 1, ks, :], raw[r][:, ks, :], w[r][:, 0, ks, :].bitcast(F32),
                                    ALU.subtract).then_inc(w_lo, 1)

            def x_low(s):
                for k in range(KD):
                    dve.wait_ge(x_hi, KD * s + k + 1)
                    v.scalar_tensor_tensor(xT[:, 1, k, :], ring[k % BANKS][:], g2[:, k:k + 1],
                                           xT[:, 0, k, :].bitcast(F32), ALU.mult, ALU.subtract).then_inc(bank_free, 1)

            def act_low(n, at, width):
                r = at % 2
                dve.wait_ge(act_hi, n + 1)
                v.tensor_tensor(actT[:, 1, at, 0:width], up[r][:, 0:width], actT[:, 0, at, 0:width].bitcast(F32),
                                ALU.subtract).then_inc(act_lo, 1)

            def body(s, width):
                e = table_entry(dve, keep, s, EXPERT, E - 1)
                dve.wait_ge(up_ready, 2 * FB * s)
                v.tensor_copy(bias[:].unsqueeze(1), bgu[:, bass.ds(e, 1), :]).then_inc(bias_ready, 1)
                dve.wait_ge(bias_ready, s + 1)
                for c in range(CH):
                    split_lo(s, c + 1)
                    half = c // 2
                    if c == 2:
                        dve.wait_ge(idx_in, 16 * s + 16)
                        dve.wait_ge(x_in, 16 * ST * s + 16 * ST)
                        dve.wait_ge(y_out, 32 * ST * s)
                        v.tensor_copy(dest[:], idx[:, :, 1:3]).then_inc(dest_ready, 1)
                    for fb in range(FB if c < 4 else 0):
                        n = 2 * FB * s + FB * half + fb
                        at = FB * half + fb
                        use = KD + USES * s + FB * c + fb
                        if c % 2 == 0:
                            dve.wait_ge(bank_full, use + 1)
                            dve.wait_ge(act_ready, n + 1 - FB if half else 2 * FB * s)
                            v.tensor_scalar(gate[:, fb, 0:width], ring[fb][:, 0:width], bias[:, at:at + 1], LIMIT,
                                            ALU.add, ALU.min).then_inc(bank_free, 1)
                        else:
                            dve.wait_ge(bank_full, use + 1)
                            if at >= 2:
                                act_low(n - 2, at - 2, width)
                            dve.wait_ge(act_lo, n - 1 if at >= 2 else 2 * FB * s)
                            v.tensor_scalar(up[fb % 2][:, 0:width], ring[fb][:, 0:width],
                                            bias[:, 2 * FB + at:2 * FB + at + 1], -LIMIT, ALU.add, ALU.max
                                            ).then_inc(bank_free, 1)
                            dve.wait_ge(bank_free, use + 1)
                            v.tensor_scalar(up[fb % 2][:, 0:width], up[fb % 2][:, 0:width], LIMIT, 1.0,
                                            ALU.min, ALU.add).then_inc(up_ready, 1)
                    if c == 3:
                        act_low(2 * FB * s + 2 * FB - 2, 2 * FB - 2, width)
                        act_low(2 * FB * s + 2 * FB - 1, 2 * FB - 1, width)
                        x_low(s + 1)

            for b in range(BANKS):
                last = v.memset(ring[b][:], 0.0)
            last.then_inc(banks_zeroed, 1)
            dve.wait_ge(g2_in, 16)
            dve.wait_ge(bgu_in, 16)
            x_low(0)
            split_lo(0, 0)
            over_slots(dve, keep, TILE_CLASS, TILE_WIDTHS, body)


def combine_stage(nc, io, scratch, keep, out):
    with ExitStack() as ctx:
        sb = lambda s, shape, dt=F32: ctx.enter_context(nc.sbuf_tensor(f"co_{s}", shape, dt))
        ps = lambda s, shape: ctx.enter_context(nc.psum_tensor(f"co_ps_{s}", shape, F32))
        sem = stage_semaphores(nc, ctx, "co")
        y4 = [sb(f"y{p}", [P, TOPK, D]) for p in range(2)]
        ht = [sb(f"h{p}", [P, D]) for p in range(2)]
        own = [sb(f"own{p}", [P, E]) for p in range(2)]
        ownT, down_bias = sb("ownT", [E, P]), sb("down_bias", [E, D])
        acc = [sb(f"acc{p}", [P, D]) for p in range(2)]
        squares, scaled = sb("squares", [P, D]), sb("scaled", [P, D])
        stat, work = sb("stat", [P, 2, 2]), sb("work", [P, ROOT_WORK, 1])
        gains = sb("gains", [P, D])
        result = [sb(f"result{p}", [P, D]) for p in range(2)]
        psT = ps("t", [E, P])
        psB = [ps(f"b{n}", [P, W]) for n in range(2)]

        y_in, h_in, result_out = ([sem(f"{s}{p}") for p in range(2)] for s in ("y_in", "h_in", "result_out"))
        bias_in, gains_in = sem("bias_in"), sem("gains_in")
        own_ready, own_turned, ownT_ready, bias_done = (sem(s) for s in ("own_ready", "own_turned", "ownT_ready", "bias_done"))
        sums, squares_ready, root_steps, rstd_ready = (sem(s) for s in ("sums", "squares_ready", "root_steps", "rstd_ready"))
        scaled_ready, result_ready = sem("scaled_ready"), sem("result_ready")
        SUMS = 2 + TOPK
        block = ctx.enter_context(nc.Block())

        @block.sync
        def _(sp):
            def store(tile):
                sp.wait_ge(result_ready, tile.t + 1)
                sp.dma_start(out[tile.rows, :], result[tile.p][:]).then_inc(result_out[tile.p], 16)

            def body(tile):
                wait(sp, sums, SUMS * (tile.t - 1))
                sp.dma_start(ht[tile.p][:], scratch["h"][tile.rows, :]).then_inc(h_in[tile.p], 16)
                sp.dma_start(y4[tile.p][:].rearrange("p k d -> p (k d)"), scratch["y"][
                    bass.ds(tile.t * P * TOPK, P * TOPK), :].rearrange("(p k) d -> p (k d)", k=TOPK)
                    ).then_inc(y_in[tile.p], 16)
                if tile.has(-2):
                    store(tile.at(-2))

            sp.dma_start(down_bias[:], io["b_down"]).then_inc(bias_in, 16)
            sp.dma_start(gains[:], io["normf_g"].to_broadcast([P, D])).then_inc(gains_in, 16)
            over_tiles(sp, body)
            store(Tile(T // 2 - 1, 0))
            store(Tile(T // 2 - 1, 1))
            for p in range(2):
                sp.wait_ge(result_out[p], 16 * (T // 2))

        @block.gpsimd
        def _(pool):
            def finish(tile):
                pool.wait_ge(scaled_ready, tile.t + 1)
                wait(pool, result_out[tile.p], 16 * tile.i)
                nc.gpsimd.tensor_tensor(result[tile.p][:], scaled[:], gains[:], ALU.mult).then_inc(result_ready, 1)

            pool.wait_ge(gains_in, 16)
            over_tiles(pool, finish)

        @block.tensor
        def _(pe):
            def body(tile):
                pe.wait_ge(own_ready, tile.t + 1)
                wait(pe, ownT_ready, tile.t)
                pe.transpose(psT[:], own[tile.p][:], keep["ident"][:]).then_inc(own_turned, 1)
                pe.wait_ge(ownT_ready, tile.t + 1)
                wait(pe, sums, SUMS * tile.t - TOPK)
                for n in range(2):
                    ins = pe.matmul(psB[n][:], ownT[:], down_bias[:, n * W:(n + 1) * W], start=True, stop=True)
                ins.then_inc(bias_done, 1)
            pe.wait_ge(bias_in, 16)
            over_tiles(pe, body)

        @block.scalar
        def _(act):
            def body(tile):
                act.wait_ge(own_turned, tile.t + 1)
                wait(act, bias_done, tile.t)
                nc.scalar.copy(ownT[:], psT[:]).then_inc(ownT_ready, 1)
                if tile.has(-1):
                    scale(tile.at(-1))

            def scale(tile):
                act.wait_ge(rstd_ready, tile.t + 1)
                wait(act, result_ready, tile.t)
                nc.scalar.mul(scaled[:], acc[tile.p][:], stat[:, tile.p, 1:2]).then_inc(scaled_ready, 1)

            over_tiles(act, body)
            scale(Tile(T // 2 - 1, 1))

        @block.vector
        def _(dve):
            v = nc.vector

            def own_gates(tile):
                wait(dve, own_turned, tile.t - 1)
                v.tensor_copy(own[tile.p][:].unsqueeze(1), keep["spread"][:, bass.ds(tile.t, 1), :]
                              ).then_inc(own_ready, 1)

            def body(tile):
                p, t = tile.p, tile.t
                c = Chain(dve, sums, SUMS * t)
                if tile.has(1):
                    own_gates(tile.at(1))
                dve.wait_ge(h_in[p], 16 * tile.i + 16)
                dve.wait_ge(bias_done, t + 1)
                wait(dve, scaled_ready, t - 1)
                v.tensor_tensor(acc[p][:, 0:W], psB[0][:], ht[p][:, 0:W], ALU.add).then_inc(sums, 1)
                v.tensor_tensor(acc[p][:, W:D], psB[1][:], ht[p][:, W:D], ALU.add).then_inc(sums, 1)
                c.n = 2
                dve.wait_ge(sums, SUMS * t + 2)
                dve.wait_ge(y_in[p], 16 * tile.i + 16)
                for k in range(TOPK):
                    c.then(v.scalar_tensor_tensor(
                        acc[p][:], y4[p][:, k, :], keep["gates"][:, bass.ds(t, 1), k:k + 1].rearrange("p a b -> p (a b)"),
                        acc[p][:], ALU.mult, ALU.add))
                v.tensor_tensor_reduce(squares[:], acc[p][:], acc[p][:], 1.0, 0.0, ALU.mult, ALU.add, stat[:, p, 0:1]
                                       ).then_inc(squares_ready, 1)
                dve.wait_ge(squares_ready, t + 1)
                inverse_root(nc, Chain(dve, root_steps, ROOT_STEPS * t), 1.0 / D, stat[:, p, 0:1], work[:],
                             stat[:, p, 1:2]).then_inc(rstd_ready, 1)
                dve.wait_ge(rstd_ready, t + 1)

            own_gates(Tile(0, 0))
            over_tiles(dve, body)


def decoder_block(nc, io, out, last="combine"):
    scratch = {
        "a": nc.dram_tensor("a_out", (S, W), F32).ap(),
        "v": nc.dram_tensor("values", (S, W), F32).ap(),
        "o": nc.dram_tensor("branches", (3, S, OROW), F32).ap(),
        "h": nc.dram_tensor("hidden", (S, D), F32).ap(),
        "hn": nc.dram_tensor("hidden_scaled", (S, D), F32).ap(),
        "list": nc.dram_tensor("slot_tokens", (LIST_ROWS, LROW), U32).ap(),
        "y": nc.dram_tensor("expert_rows", (S * TOPK + LIST_ROWS, D), F32).ap(),
        "table": nc.dram_tensor("slot_table", (NSLOTS + 1, ENTRY), I32).ap(),
    }
    with ExitStack() as ctx:
        keep = {
            "ident": ctx.enter_context(nc.sbuf_tensor("ident", [P, P], F32)),
            "ident_in": ctx.enter_context(nc.semaphore("ident_in")),
        }
        for name, shape, dt in (("posn", [P, T, TOPK], U32), ("gates", [P, T, TOPK], F32),
                                ("spread", [P, T, E], F32), ("table", [1, ENTRY * (NSLOTS + 1)], I32)):
            keep[name] = ctx.enter_context(nc.sbuf_tensor(name, shape, dt))
        with nc.Block() as block:
            @block.sync
            def _(sp):
                sp.dma_start(keep["ident"][:], io["ident"]).then_inc(keep["ident_in"], 16)
        gating_stage(nc, io, scratch, keep)
        with ExitStack() as heads:
            for name in ("qT", "kT"):
                keep[name] = heads.enter_context(nc.sbuf_tensor(name, [P, PAIRS, S], F32))
            rotary_stage(nc, io, scratch, keep)
            attention_stage(nc, io, scratch, keep)
        if last == "attention":
            return
        with nc.sbuf_tensor("logits", [P, T, E], F32) as keep["logits"]:
            mixing_stage(nc, io, scratch, keep)
            if last == "mixing":
                return
            routing_stage(nc, io, scratch, keep)
        if last == "routing":
            return
        experts_stage(nc, io, scratch, keep)
        combine_stage(nc, io, scratch, keep, out)


_LAYOUT = {
    "x": lambda a: a.reshape(S, D),
    "norm1_g": lambda a: a.reshape(KD, P).T,
    "w_in": lambda a: a.reshape(D, -1),
    "a_ln_g": lambda a: a.reshape(1, W),
    "a_ln_b": lambda a: a.reshape(1, W),
    "a_w_s": lambda a: a.reshape(H, P, P).transpose(2, 0, 1),
    "a_b_s": lambda a: a.reshape(H, P).T,
    "w_out": lambda a: a.reshape(D, D),
    "norm2_g": lambda a: a.reshape(KD, P).T,
    "w_router": lambda a: a.reshape(KD, P, E).transpose(1, 0, 2),
    "b_router": lambda a: a.reshape(1, E),
    "w_gate_up": lambda a: a.reshape(E, D, 2 * FF),
    "b_gate_up": lambda a: a.reshape(E, 2 * FF // P, P).transpose(2, 0, 1),
    "w_down": lambda a: a.reshape(E, FF, D),
    "b_down": lambda a: a.reshape(E, D),
    "normf_g": lambda a: a.reshape(1, D),
}


def _constants():
    import numpy as np
    f = np.float32
    inv = f(10000.0) ** (-np.arange(0, DH, 2, dtype=f) / f(DH))
    angle = np.arange(S, dtype=f)[:, None] * inv[None, :]
    cos, sin = np.cos(angle), np.sin(angle)
    at = np.arange(P)
    before, here = at[None, :] < at[:, None], at[None, :] > at[:, None]
    band = np.where(np.concatenate([before, here], 1), f(-1e30), f(0))
    return {
        "ident": np.eye(P, dtype=f),
        "rope": np.stack([np.concatenate([cos, cos], 1), np.concatenate([-sin, sin], 1)], 1).astype(f),
        "tri": (at[:, None] <= at[None, :]).astype(f),
        "before": (at[:, None] < at[None, :]).astype(f),
        "band": band.astype(f),
        "token": (np.arange(T)[None, :] * P + at[:, None]).astype(f),
        "expert": np.arange(E, dtype=f)[None, :],
        "slot": np.arange(P, dtype=f)[:, None],
    }


def kernel(**inputs):
    import numpy as np
    import concourse.bacc as bacc
    from concourse.bass_utils import run_bass_kernel_spmd

    nc = bacc.Bacc("TRN2", target_bir_lowering=False, num_devices=1)
    arrays = {name: np.ascontiguousarray(lay(np.asarray(inputs[name]))) for name, lay in _LAYOUT.items()}
    gains = np.concatenate([np.asarray(inputs["a_out_g"]).reshape(W), np.asarray(inputs["b_out_g"]).reshape(W)])
    arrays["mix_g"] = np.ascontiguousarray(gains.reshape(KD, P).T)
    arrays.update(_constants())
    io = {name: nc.dram_tensor(f"in_{name}", a.shape, mybir.dt.from_np(a.dtype), kind="ExternalInput").ap()
          for name, a in arrays.items()}
    out = nc.dram_tensor("out", (S, D), F32, kind="ExternalOutput").ap()
    decoder_block(nc, io, out)
    done = run_bass_kernel_spmd(nc, [{f"in_{name}": a for name, a in arrays.items()}], core_ids=[0])
    return done.results[0]["out"].reshape(1, S, D)
```

```python
from contextlib import ExitStack

import concourse.bass as bass
from concourse import mybir

F32 = mybir.dt.float32
F32R = mybir.dt.float32r
BF16 = mybir.dt.bfloat16
I32 = mybir.dt.int32
U32 = mybir.dt.uint32
ALU = mybir.AluOpType
ACT = mybir.ActivationFunctionType
AX = mybir.AxisListType

P = 128
S = 2048
D = 1024
T = S // P
KD = D // P
H = 8
DH = 64
W = H * DH
PAIRS = H // 2
E = 32
TOPK = 4
FF = D
SLOT = 512
ST = SLOT // P
NSLOTS = (S * TOPK + E * (SLOT - 1)) // SLOT
EPS = 1e-5
SCALE = DH ** -0.5
ALPHA = 1.702
LIMIT = 7.0
OROW = W + 2 * H
DILATIONS = (1, 4, 16)
COLS = (NSLOTS + 1) * ST
LIST_STRIDE = 512
P_BITS = P.bit_length() - 1
SPLIT3 = ((0, 0), (0, 1), (1, 0))


def stage_semaphores(nc, ctx, name):
    used = []

    def clear():
        nc.clear_and_free_semaphores(used)
        nc.all_engine_barrier()

    def sem(s):
        used.append(nc.alloc_semaphore(f"{name}_{s}"))
        return used[-1]

    ctx.callback(clear)
    return sem


def wait(eng, sem, value):
    if not isinstance(value, int) or value > 0:
        eng.wait_ge(sem, value)


class Chain:

    def __init__(self, eng, sem, base):
        self.eng, self.sem, self.base, self.n = eng, sem, base, 0

    def then(self, ins):
        ins.then_inc(self.sem, 1)
        self.n += 1
        self.eng.wait_ge(self.sem, self.base + self.n)


ROOT_STEPS = 10
ROOT_WORK = 4
ROOT_GUESS = 0x5F3759DF


def inverse_root(nc, chain, value, sums, work, out):
    v = nc.vector
    mean, neg_half, t, y = (work[:, n, :] for n in range(4))
    chain.then(v.tensor_scalar(mean, sums, value, EPS, ALU.mult, ALU.add))
    v.tensor_scalar(neg_half, mean, -0.5, None, ALU.mult)
    chain.then(v.tensor_scalar(y.bitcast(I32), mean.bitcast(I32), -0.5, float(ROOT_GUESS), ALU.mult, ALU.add))
    for turn in range(3):
        chain.then(v.tensor_tensor(t, y, y, ALU.mult))
        chain.then(v.tensor_tensor(t, t, neg_half, ALU.mult))
        last = v.scalar_tensor_tensor(out if turn == 2 else y, t, 1.5, y, ALU.add, ALU.mult)
        if turn < 2:
            chain.then(last)
    assert chain.n == ROOT_STEPS
    return last


class Tile:

    def __init__(self, i, p):
        self.i, self.p, self.t = i, p, 2 * i + p
        self.rows = bass.ds(self.t * P, P)

    def has(self, d):
        return not isinstance(self.t, int) or 0 <= self.t + d < T

    def at(self, d):
        j = self.p + d
        return Tile(self.i + j // 2, j % 2)


def over_tiles(eng, body, ahead=2, peeled=1):
    last = T // 2 - (ahead + 1) // 2
    for i in range(peeled):
        for p in range(2):
            body(Tile(i, p))
    with eng.Fori(peeled, last) as i:
        for p in range(2):
            body(Tile(i, p))
    for i in range(last, T // 2):
        for p in range(2):
            body(Tile(i, p))


class Front:

    def __init__(self, nc, ctx, sem, name, keep, g_cols, w_dram, groups, rows=None):
        self.nc, self.w_dram, self.groups, self.ident = nc, w_dram, groups, keep["ident"]
        sb = lambda s, shape, dt=F32: ctx.enter_context(nc.sbuf_tensor(f"{name}_{s}", shape, dt))
        n = len(groups)
        self.xn = [sb("xn", [P, D])] * 2 if rows is None else rows
        self.xT = [sb(f"xT{p}", [P, 2, KD, P], F32R) for p in range(2)]
        self.raw = [sb(f"raw{r}", [P, KD, W]) for r in range(2)]
        self.w = [sb(f"w{g}", [P, 2, KD, W], F32R) for g in range(n)]
        self.g = sb("g", [P, KD])
        self.psT = ctx.enter_context(nc.psum_tensor(f"{name}_psT", [P, KD, P], F32))
        self.g_dram = g_cols
        self.g_in = sem("g_in")
        self.raw_in = [sem(f"raw_in{g}") for g in range(n)]
        self.w_hi, self.w_lo = sem("w_hi"), sem("w_lo")
        self.xn_ready = sem("xn_ready")
        self.turned = sem("turned")
        self.hi_ready, self.lo_ready = sem("hi_ready"), sem("lo_ready")
        self.gemm_done = sem("gemm_done")

    def load_gains(self, sp):
        sp.dma_start(self.g[:], self.g_dram).then_inc(self.g_in, 16)

    def load_weights(self, sp, first=0, last=None):
        for n in range(first, len(self.groups) if last is None else last):
            c0 = self.groups[n]
            if n >= 2:
                sp.wait_ge(self.w_lo, n - 1)
            sp.dma_start(self.raw[n % 2][:], self.w_dram[:, c0:c0 + W].rearrange("(k p) n -> p k n", p=P)
                         ).then_inc(self.raw_in[n], 16)

    def weights_hi(self, act, *groups):
        for n in groups:
            act.wait_ge(self.raw_in[n], 16)
            self.nc.scalar.copy(self.w[n][:, 0], self.raw[n % 2][:]).then_inc(self.w_hi, 1)

    def hi_x(self, act, tile):
        act.wait_ge(self.turned, tile.t + 1)
        wait(act, self.gemm_done, tile.t - 1)
        for k in range(KD):
            ins = self.nc.scalar.mul(self.xT[tile.p][:, 0, k, :], self.psT[:, k, :], self.g[:, k:k + 1])
        ins.then_inc(self.hi_ready, 1)

    def weights_lo(self, dve, *groups):
        for n in groups:
            dve.wait_ge(self.w_hi, n + 1)
            self.nc.vector.tensor_tensor(self.w[n][:, 1], self.raw[n % 2][:], self.w[n][:, 0].bitcast(F32),
                                         ALU.subtract).then_inc(self.w_lo, 1)

    def lo_x(self, dve, tile):
        dve.wait_ge(self.hi_ready, tile.t + 1)
        for k in range(KD):
            ins = self.nc.vector.scalar_tensor_tensor(
                self.xT[tile.p][:, 1, k, :], self.psT[:, k, :], self.g[:, k:k + 1],
                self.xT[tile.p][:, 0, k, :].bitcast(F32), ALU.mult, ALU.subtract)
        ins.then_inc(self.lo_ready, 1)

    def turn_x(self, pe, tile):
        pe.wait_ge(self.xn_ready, tile.t + 1)
        wait(pe, self.lo_ready, tile.t)
        for k in range(KD):
            ins = pe.transpose(self.psT[:, k, :], self.xn[tile.p][:, k * P:(k + 1) * P], self.ident[:])
        ins.then_inc(self.turned, 1)

    def gemm(self, pe, tile, n, out):
        if isinstance(tile.t, int) and tile.t == 0:
            pe.wait_ge(self.w_lo, n + 1)
        m = 0
        for k in range(KD):
            for a, b in SPLIT3:
                ins = pe.matmul(out, self.xT[tile.p][:, a, k, :], self.w[n][:, b, k, :],
                                start=(m == 0), stop=(m == 3 * KD - 1))
                m += 1
        return ins


class NormFront(Front):

    def __init__(self, nc, ctx, sem, name, keep, x, g_cols, w_dram, groups):
        super().__init__(nc, ctx, sem, name, keep, g_cols, w_dram, groups)
        sb = lambda s, shape, dt=F32: ctx.enter_context(nc.sbuf_tensor(f"{name}_{s}", shape, dt))
        self.x = x
        self.xt = [sb(f"x{p}", [P, D]) for p in range(2)]
        self.squares = sb("squares", [P, D])
        self.stat, self.work = sb("stat", [P, 2, 2]), sb("work", [P, ROOT_WORK, 1])
        self.x_in = [sem(f"x_in{p}") for p in range(2)]
        self.rstd_ready = sem("rstd_ready")
        self.squares_ready, self.root_steps = sem("squares_ready"), sem("root_steps")

    def load_x(self, sp, tile):
        wait(sp, self.xn_ready, tile.t - 1)
        sp.dma_start(self.xt[tile.p][:], self.x[tile.rows, :]).then_inc(self.x_in[tile.p], 16)

    def scale_x(self, act, tile):
        act.wait_ge(self.rstd_ready, tile.t + 1)
        wait(act, self.turned, tile.t)
        self.nc.scalar.mul(self.xn[tile.p][:], self.xt[tile.p][:], self.stat[:, tile.p, 1:2]
                           ).then_inc(self.xn_ready, 1)

    def sum_squares(self, dve, tile):
        v, st, p = self.nc.vector, self.stat, tile.p
        dve.wait_ge(self.x_in[p], 16 * tile.i + 16)
        wait(dve, self.xn_ready, tile.t - 1)
        v.tensor_tensor_reduce(self.squares[:], self.xt[p][:], self.xt[p][:], 1.0, 0.0,
                               ALU.mult, ALU.add, st[:, p, 0:1]).then_inc(self.squares_ready, 1)

    def rstd(self, dve, tile):
        self.sum_squares(dve, tile)
        dve.wait_ge(self.squares_ready, tile.t + 1)
        inverse_root(self.nc, Chain(dve, self.root_steps, ROOT_STEPS * tile.t), 1.0 / D,
                     self.stat[:, tile.p, 0:1], self.work[:], self.stat[:, tile.p, 1:2]
                     ).then_inc(self.rstd_ready, 1)


def gating_stage(nc, io, scratch, keep):
    with ExitStack() as ctx:
        sb = lambda s, shape, dt=F32: ctx.enter_context(nc.sbuf_tensor(f"ga_{s}", shape, dt))
        ps = lambda s, shape: ctx.enter_context(nc.psum_tensor(f"ga_ps_{s}", shape, F32))
        sem = stage_semaphores(nc, ctx, "ga")
        AV, V, U = 0, 1, 2
        f = NormFront(nc, ctx, sem, "ga", keep, io["x"], io["norm1_g"], io["w_in"], (W, 4 * W, 0))
        ident = keep["ident"]
        gains, biases = sb("ln_g", [P, W]), sb("ln_b", [P, W])
        ws, tri, bs = sb("ws", [P, H, P]), sb("tri", [P, P]), sb("bs", [P, H])
        vg, vc, vq, vn = (sb(s, [P, H, DH]) for s in ("vg", "vc", "vq", "vn"))
        ug = [sb(f"ug{p}", [P, H, DH]) for p in range(2)]
        gt, a = sb("gt", [P, H, DH]), sb("a", [P, H, DH])
        an = [sb(f"an{p}", [P, W]) for p in range(2)]
        vo = [sb(f"vo{p}", [P, W]) for p in range(2)]
        ln, ast = sb("ln", [P, 4, H]), sb("ast", [P, 2])
        ln_work, a_work = sb("ln_work", [P, ROOT_WORK, H]), sb("a_work", [P, ROOT_WORK, 1])
        psG = [ps(f"g{n}", [P, W]) for n in range(3)]
        psM = ps("mix", [P, H, DH])

        ws_in, tri_in, bs_in, lng_in, lnb_in = (sem(s) for s in ("ws_in", "tri_in", "bs_in", "lng_in", "lnb_in"))
        ws_masked = sem("ws_masked")
        proj_done = sem("proj_done")
        vg_ready, vo_ready, ug_ready = sem("vg_ready"), sem("vo_ready"), sem("ug_ready")
        vn_ready, mixed, combined = sem("vn_ready"), sem("mixed"), sem("combined")
        a_ready, an_ready = sem("a_ready"), sem("an_ready")
        ln_steps, bias_added = sem("ln_steps"), sem("bias_added")
        ln_root_steps, ln_rstd_ready = sem("ln_root_steps"), sem("ln_rstd_ready")
        a_squares_ready, a_root_steps = sem("a_squares_ready"), sem("a_root_steps")
        an_out = [sem(f"an_out{p}") for p in range(2)]
        vo_out = [sem(f"vo_out{p}") for p in range(2)]
        block = ctx.enter_context(nc.Block())

        @block.sync
        def _(sp):
            f.load_x(sp, Tile(0, 0))
            f.load_x(sp, Tile(0, 1))
            f.load_gains(sp)
            f.load_weights(sp, last=2)
            sp.dma_start(ws[:], io["a_w_s"]).then_inc(ws_in, 16)
            sp.dma_start(tri[:], io["tri"]).then_inc(tri_in, 16)
            sp.dma_start(bs[:], io["a_b_s"]).then_inc(bs_in, 16)
            sp.dma_start(gains[:], io["a_ln_g"].to_broadcast([P, W])).then_inc(lng_in, 16)
            sp.dma_start(biases[:], io["a_ln_b"].to_broadcast([P, W])).then_inc(lnb_in, 16)
            f.load_weights(sp, first=2)
            with sp.Fori(1, T // 2) as i:
                for p in range(2):
                    f.load_x(sp, Tile(i, p))

        @block.tensor
        def _(pe):
            def gate(tile):
                if isinstance(tile.t, int) and tile.t == 0:
                    pe.wait_ge(ws_masked, 1)
                pe.wait_ge(vn_ready, tile.t + 1)
                wait(pe, combined, tile.t)
                for h in range(H):
                    ins = pe.matmul(psM[:, h, :], ws[:, h, :], vn[:, h, :], start=True, stop=True)
                ins.then_inc(mixed, 1)

            def body(tile):
                if tile.has(1):
                    f.turn_x(pe, tile.at(1))
                pe.wait_ge(f.lo_ready, tile.t + 1)
                for n, read in ((AV, vg_ready), (V, vo_ready), (U, ug_ready)):
                    wait(pe, read, tile.t)
                    ins = f.gemm(pe, tile, n, psG[n][:])
                    ins.then_inc(proj_done if n != U else f.gemm_done, 1)
                if tile.has(-1):
                    gate(tile.at(-1))

            pe.wait_ge(keep["ident_in"], 16)
            f.turn_x(pe, Tile(0, 0))
            over_tiles(pe, body)
            gate(Tile(T // 2 - 1, 1))

        @block.scalar
        def _(act):
            def finish(tile):
                act.wait_ge(a_ready, tile.t + 1)
                wait(act, an_out[tile.p], 16 * tile.i)
                nc.scalar.mul(an[tile.p][:], a[:].rearrange("p h d -> p (h d)"), ast[:, 1:2]
                              ).then_inc(an_ready, 1)
                act.wait_ge(vo_ready, tile.t + 1)
                act.dma_start(scratch["v"][tile.rows, :], vo[tile.p][:]).then_inc(vo_out[tile.p], 16)
                act.wait_ge(an_ready, tile.t + 1)
                act.dma_start(scratch["a"][tile.rows, :], an[tile.p][:]).then_inc(an_out[tile.p], 16)

            def body(tile):
                p, t = tile.p, tile.t
                if tile.has(1):
                    f.hi_x(act, tile.at(1))
                act.wait_ge(proj_done, 2 * t + 1)
                wait(act, vn_ready, t)
                nc.scalar.activation(vg[:].rearrange("p h d -> p (h d)"), psG[AV][:], ACT.Gelu_apprx_tanh
                                     ).then_inc(vg_ready, 1)
                act.wait_ge(proj_done, 2 * t + 2)
                wait(act, vo_out[p], 16 * tile.i)
                nc.scalar.copy(vo[p][:], psG[V][:]).then_inc(vo_ready, 1)
                act.wait_ge(f.gemm_done, t + 1)
                wait(act, combined, t - 1)
                nc.scalar.activation(ug[p][:].rearrange("p h d -> p (h d)"), psG[U][:], ACT.Gelu_apprx_tanh
                                     ).then_inc(ug_ready, 1)
                if tile.has(2):
                    f.scale_x(act, tile.at(2))
                if tile.has(-1):
                    finish(tile.at(-1))

            act.wait_ge(f.g_in, 16)
            f.scale_x(act, Tile(0, 0))
            f.weights_hi(act, 0)
            f.hi_x(act, Tile(0, 0))
            f.scale_x(act, Tile(0, 1))
            f.weights_hi(act, *range(1, len(f.groups)))
            over_tiles(act, body, peeled=2)
            finish(Tile(T // 2 - 1, 1))
            for p in range(2):
                act.wait_ge(vo_out[p], 16 * (T // 2))
                act.wait_ge(an_out[p], 16 * (T // 2))

        @block.vector
        def _(dve):
            v = nc.vector

            def layer_norm(tile):
                c = Chain(dve, ln_steps, 7 * tile.t)
                col = lambda n: ln[:, n, :].unsqueeze(2).to_broadcast([P, H, DH])
                flat = lambda x: x[:].rearrange("p h d -> p (h d)")
                dve.wait_ge(vg_ready, tile.t + 1)
                c.then(v.reduce_sum(ln[:, 0, :], vg[:], AX.X))
                c.then(v.tensor_scalar(ln[:, 1, :], ln[:, 0, :], 1.0 / DH, None, ALU.mult))
                c.then(v.tensor_tensor(vc[:], vg[:], col(1), ALU.subtract))
                c.then(v.tensor_tensor(vq[:], vc[:], vc[:], ALU.mult))
                c.then(v.reduce_sum(ln[:, 2, :], vq[:], AX.X))
                inverse_root(nc, Chain(dve, ln_root_steps, ROOT_STEPS * tile.t), 1.0 / DH, ln[:, 2, :],
                             ln_work[:], ln[:, 3, :]).then_inc(ln_rstd_ready, 1)
                dve.wait_ge(ln_rstd_ready, tile.t + 1)
                c.then(v.tensor_tensor(vq[:], vc[:], col(3), ALU.mult))
                c.then(v.tensor_tensor(flat(vc), flat(vq), gains[:], ALU.mult))
                wait(dve, mixed, tile.t)
                v.tensor_tensor(flat(vn), flat(vc), biases[:], ALU.add).then_inc(vn_ready, 1)

            def combine(tile):
                dve.wait_ge(mixed, tile.t + 1)
                wait(dve, a_squares_ready, tile.t)
                dve.wait_ge(ug_ready, tile.t + 1)
                v.tensor_tensor(gt[:], psM[:], bs[:].unsqueeze(2).to_broadcast([P, H, DH]), ALU.add
                                ).then_inc(bias_added, 1)
                dve.wait_ge(bias_added, tile.t + 1)
                wait(dve, an_ready, tile.t)
                v.tensor_tensor(a[:], gt[:], ug[tile.p][:], ALU.mult).then_inc(combined, 1)
                dve.wait_ge(combined, tile.t + 1)
                v.tensor_tensor_reduce(gt[:], a[:], a[:], 1.0, 0.0, ALU.mult, ALU.add, ast[:, 0:1]
                                       ).then_inc(a_squares_ready, 1)
                dve.wait_ge(a_squares_ready, tile.t + 1)
                inverse_root(nc, Chain(dve, a_root_steps, ROOT_STEPS * tile.t), 1.0 / W, ast[:, 0:1],
                             a_work[:], ast[:, 1:2]).then_inc(a_ready, 1)

            def body(tile):
                if tile.has(1):
                    f.lo_x(dve, tile.at(1))
                if tile.has(2):
                    f.rstd(dve, tile.at(2))
                layer_norm(tile)
                if tile.has(-1):
                    combine(tile.at(-1))

            dve.wait_ge(f.g_in, 16)
            f.rstd(dve, Tile(0, 0))
            f.rstd(dve, Tile(0, 1))
            f.weights_lo(dve, 0)
            f.lo_x(dve, Tile(0, 0))
            f.weights_lo(dve, *range(1, len(f.groups)))
            dve.wait_ge(ws_in, 16)
            dve.wait_ge(tri_in, 16)
            v.tensor_tensor(ws[:], ws[:], tri[:].unsqueeze(1).to_broadcast([P, H, P]), ALU.mult
                            ).then_inc(ws_masked, 1)
            for s in (bs_in, lng_in, lnb_in):
                dve.wait_ge(s, 16)
            over_tiles(dve, body)
            combine(Tile(T // 2 - 1, 1))


def rotary_stage(nc, io, scratch, keep):
    with ExitStack() as ctx:
        sb = lambda s, shape, dt=F32: ctx.enter_context(nc.sbuf_tensor(f"ro_{s}", shape, dt))
        ps = lambda s, shape: ctx.enter_context(nc.psum_tensor(f"ro_ps_{s}", shape, F32))
        sem = stage_semaphores(nc, ctx, "ro")
        f = NormFront(nc, ctx, sem, "ro", keep, io["x"], io["norm1_g"], io["w_in"], (2 * W, 3 * W))
        tab = [sb(f"tab{p}", [P, 2, DH]) for p in range(2)]
        straight, turned_half = sb("straight", [P, H, DH]), sb("turned_half", [P, H, DH])
        rot = [sb(f"rot{n}", [P, H, DH]) for n in range(2)]
        psQ = [ps(f"q{n}", [P, H, DH]) for n in range(2)]
        psR = [ps(f"r{n}", [P, PAIRS, P]) for n in range(2)]
        tab_in = [sem(f"tab_in{p}") for p in range(2)]
        q_done = sem("q_done")
        products = sem("products")
        rot_ready = sem("rot_ready")
        heads_turned = sem("heads_turned")
        heads_kept = sem("heads_kept")
        block = ctx.enter_context(nc.Block())

        @block.sync
        def _(sp):
            def load(tile):
                f.load_x(sp, tile)
                wait(sp, rot_ready, 2 * tile.t - 2)
                sp.dma_start(tab[tile.p][:], io["rope"][tile.rows, :, :]).then_inc(tab_in[tile.p], 16)
            load(Tile(0, 0))
            load(Tile(0, 1))
            f.load_gains(sp)
            f.load_weights(sp)
            with sp.Fori(1, T // 2) as i:
                for p in range(2):
                    load(Tile(i, p))

        @block.gpsimd
        def _(pool):
            def add_halves(tile):
                for n in range(2):
                    pool.wait_ge(products, 2 * tile.t + n + 1)
                    wait(pool, heads_turned, tile.t)
                    nc.gpsimd.tensor_tensor(rot[n][:], straight[:], turned_half[:], ALU.add
                                            ).then_inc(rot_ready, 1)

            over_tiles(pool, add_halves)

        @block.tensor
        def _(pe):
            def turn_heads(tile):
                pe.wait_ge(rot_ready, 2 * tile.t + 2)
                wait(pe, heads_kept, 2 * tile.t)
                for n in range(2):
                    for pr in range(PAIRS):
                        ins = pe.transpose(psR[n][:, pr, :], rot[n][:, 2 * pr:2 * pr + 2, :].rearrange(
                            "p h d -> p (h d)"), keep["ident"][:])
                ins.then_inc(heads_turned, 1)

            def body(tile):
                if tile.has(1):
                    f.turn_x(pe, tile.at(1))
                pe.wait_ge(f.lo_ready, tile.t + 1)
                for n in range(2):
                    wait(pe, products, 2 * tile.t - 1 + n)
                    ins = f.gemm(pe, tile, n, psQ[n][:].rearrange("p h d -> p (h d)"))
                    ins.then_inc(f.gemm_done if n else q_done, 1)
                if tile.has(-1):
                    turn_heads(tile.at(-1))

            f.turn_x(pe, Tile(0, 0))
            over_tiles(pe, body)
            turn_heads(Tile(T // 2 - 1, 1))

        @block.scalar
        def _(act):
            def keep_heads(tile):
                act.wait_ge(heads_turned, tile.t + 1)
                for n, kept in enumerate((keep["qT"], keep["kT"])):
                    nc.scalar.copy(kept[:, :, tile.rows], psR[n][:]).then_inc(heads_kept, 1)

            def body(tile):
                if tile.has(1):
                    f.hi_x(act, tile.at(1))
                if tile.has(2):
                    f.scale_x(act, tile.at(2))
                if tile.has(-1):
                    keep_heads(tile.at(-1))

            act.wait_ge(f.g_in, 16)
            f.scale_x(act, Tile(0, 0))
            f.weights_hi(act, 0)
            f.hi_x(act, Tile(0, 0))
            f.scale_x(act, Tile(0, 1))
            f.weights_hi(act, *range(1, len(f.groups)))
            over_tiles(act, body)
            keep_heads(Tile(T // 2 - 1, 1))

        @block.vector
        def _(dve):
            v, half = nc.vector, DH // 2

            def rotate(tile):
                p = tile.p
                dve.wait_ge(tab_in[p], 16 * tile.i + 16)
                table = lambda n, lo, hi: tab[p][:, n, lo:hi].unsqueeze(1).to_broadcast([P, H, hi - lo])
                for n in range(2):
                    if n:
                        dve.wait_ge(f.gemm_done, tile.t + 1)
                    else:
                        dve.wait_ge(q_done, tile.t + 1)
                    wait(dve, rot_ready, 2 * tile.t + n)
                    v.tensor_tensor(straight[:], psQ[n][:], table(0, 0, DH), ALU.mult)
                    v.tensor_tensor(turned_half[:, :, 0:half], psQ[n][:, :, half:DH], table(1, 0, half), ALU.mult)
                    v.tensor_tensor(turned_half[:, :, half:DH], psQ[n][:, :, 0:half], table(1, half, DH), ALU.mult
                                    ).then_inc(products, 1)

            def body(tile):
                if tile.has(1):
                    f.lo_x(dve, tile.at(1))
                if tile.has(2):
                    f.rstd(dve, tile.at(2))
                rotate(tile)

            dve.wait_ge(f.g_in, 16)
            f.rstd(dve, Tile(0, 0))
            f.rstd(dve, Tile(0, 1))
            f.weights_lo(dve, 0)
            f.lo_x(dve, Tile(0, 0))
            f.weights_lo(dve, *range(1, len(f.groups)))
            over_tiles(dve, body)


class AttentionBlock:

    def __init__(self, branch, g, j):
        self.branch, self.g, self.j = branch, g, j
        self.dil = DILATIONS[branch]
        self.b = 4 * g + j
        self.n = 16 * branch + self.b
        if branch == 0:
            start = self.b * P
            self.has_prev = not (isinstance(g, int) and g == 0 and j == 0)
        elif branch == 1:
            start = g + j * P * self.dil
            self.has_prev = j > 0
        else:
            start = self.b
            self.has_prev = False
        self.tokens = bass.ds(start, P, self.dil)
        self.c0 = 0 if self.has_prev else 1


def over_groups(eng, body):
    before = []
    for branch in range(len(DILATIONS)):
        group_of = lambda g: [AttentionBlock(branch, g, j) for j in range(4)]
        body(group_of(0), before)
        with eng.Fori(1, 4) as g:
            body(group_of(g), group_of(g - 1)[2:])
        before = group_of(3)[2:]
    return before


def attention_stage(nc, io, scratch, keep):
    with ExitStack() as ctx:
        sb = lambda s, shape, dt=F32: ctx.enter_context(nc.sbuf_tensor(f"at_{s}", shape, dt))
        ps = lambda s, shape: ctx.enter_context(nc.psum_tensor(f"at_ps_{s}", shape, F32))
        sem = stage_semaphores(nc, ctx, "at")
        qb = [sb(f"q{r}", [P, 2, PAIRS, P], F32R) for r in range(2)]
        kb = sb("k", [P, 2, PAIRS, 4, P], F32R)
        vb = [sb(f"v{r}", [P, W]) for r in range(4)]
        mask_in_f32, identb, mask = sb("mask_f32", [P, 2 * P]), sb("identb", [P, P], BF16), sb("mask", [P, 2 * P], BF16)
        prob = [sb(f"p{u}", [P, 2, 2, 2 * P]) for u in range(2)]
        probT = [sb(f"pT{u}", [P, 2, 2, 2, P]) for u in range(2)]
        top = [sb(f"top{u}", [P, 2, 2]) for u in range(2)]
        ob = [sb(f"o{r}", [P, OROW]) for r in range(4)]
        psS = [ps(f"s{u}", [P, 2, 2, 2 * P]) for u in range(2)]
        psT = ps("t", [P, 2, 2, 2, P])
        psO = [ps(f"o{r}", [P, W]) for r in range(2)]

        mask_in, mask_ready = sem("mask_in"), sem("mask_ready")
        v_in = [sem(f"v_in{r}") for r in range(4)]
        blocks_hi, rest_go, blocks_split = sem("blocks_hi"), sem("rest_go"), sem("blocks_split")
        scores_ready, top_ready, negmax_ready = sem("scores_ready"), sem("top_ready"), sem("negmax_ready")
        exp_done, probs_turned = sem("exp_done"), sem("probs_turned")
        kept_by_dve, kept_by_act = sem("kept_by_dve"), sem("kept_by_act")
        weighted = sem("weighted")
        o_ready = sem("o_ready")
        o_out = [sem(f"o_out{r}") for r in range(4)]
        block = ctx.enter_context(nc.Block())

        def units(group):
            return [(blk, u, 2 * blk.n + u) for blk in group for u in range(2)]

        def round_of(blk):
            return 4 * blk.branch + blk.g

        def head(u, half, pr):
            return 2 * (2 * u + pr) + half

        @block.sync
        def _(sp):
            sp.dma_start(mask_in_f32[:], io["band"]).then_inc(mask_in, 16)

            def body(group, before):
                for blk in group:
                    first = isinstance(blk.n, int) and blk.n < 4
                    if not first:
                        sp.wait_ge(weighted, 2 * blk.n - 4)
                    sp.dma_start(vb[blk.j][:], scratch["v"][blk.tokens, :]).then_inc(v_in[blk.j], 16)
            over_groups(sp, body)

        @block.gpsimd
        def _(pool):
            def body(group, before):
                for blk in group:
                    if not (isinstance(blk.n, int) and blk.n < 2):
                        pool.wait_ge(scores_ready, 2 * blk.n - 2)
                    pairs = ((qb[blk.j % 2], keep["qT"]), (kb[:, :, :, blk.j, :], keep["kT"]))
                    for split, whole in pairs:
                        nc.gpsimd.tensor_copy(split[:, 0], whole[:, :, blk.tokens]).then_inc(blocks_hi, 1)
                    for m, (split, whole) in enumerate(pairs):
                        pool.wait_ge(blocks_hi, 2 * blk.n + m + 1)
                        pool.sem_inc(rest_go, 1)
                        nc.gpsimd.tensor_tensor(split[:, 1], whole[:, :, blk.tokens], split[:, 0].bitcast(F32),
                                                ALU.subtract).then_inc(blocks_split, 1)
            over_groups(pool, body)

        @block.tensor
        def _(pe):
            def scores(blk, u, n):
                pe.wait_ge(blocks_split, 2 * blk.n + 2)
                wait(pe, exp_done, n - 1)
                cols = slice(blk.c0 * P, 2 * P)
                for half in range(2):
                    part = slice(DH * half, DH * half + DH)
                    pe.matmul(psS[u][:, half, :, cols], identb[:],
                              mask[:, cols].unsqueeze(1).to_broadcast([P, 2, (2 - blk.c0) * P]), start=True, stop=False)
                    for pr in range(2):
                        for a, b in SPLIT3:
                            last = pr == 1 and (a, b) == SPLIT3[-1]
                            query = qb[blk.j % 2][part, a, 2 * u + pr, :]
                            if blk.has_prev and blk.j > 0:
                                ins = pe.matmul(psS[u][:, half, pr, :], query,
                                                kb[part, b, 2 * u + pr, blk.j - 1:blk.j + 1, :], start=False, stop=last)
                                continue
                            for c in range(blk.c0, 2):
                                ins = pe.matmul(psS[u][:, half, pr, c * P:(c + 1) * P], query,
                                                kb[part, b, 2 * u + pr, (blk.j - 1 + c) % 4, :],
                                                start=False, stop=(last and c == 1))
                ins.then_inc(scores_ready, 1)

            def turn(blk, u, n):
                pe.wait_ge(exp_done, n + 1)
                wait(pe, kept_by_dve, n)
                wait(pe, kept_by_act, n)
                for half in range(2):
                    for pr in range(2):
                        for c in range(blk.c0, 2):
                            ins = pe.transpose(psT[:, half, pr, c, :], prob[u][:, half, pr, c * P:(c + 1) * P],
                                               keep["ident"][:])
                ins.then_inc(probs_turned, 1)

            def weigh(blk, u, n):
                pe.wait_ge(kept_by_dve, n + 1)
                pe.wait_ge(kept_by_act, n + 1)
                if u == 0:
                    wait(pe, o_ready, blk.n - 1)
                    pe.wait_ge(v_in[blk.j], 16 * round_of(blk) + 16)
                for half in range(2):
                    for pr in range(2):
                        cols = slice(DH * head(u, half, pr), DH * head(u, half, pr) + DH)
                        for c in range(blk.c0, 2):
                            ins = pe.matmul(psO[blk.j % 2][:, cols], probT[u][:, half, pr, c, :],
                                            vb[(blk.j - 1 + c) % 4][:, cols], start=(c == blk.c0), stop=(c == 1))
                ins.then_inc(weighted, 1)

            def body(group, before):
                us, old = units(before + group), 2 * len(before)
                for s in range(old, len(us)):
                    scores(*us[s])
                    if s >= 1:
                        turn(*us[s - 1])
                    if s >= 2:
                        weigh(*us[s - 2])
            pe.wait_ge(mask_ready, 2)
            us = units(over_groups(pe, body))
            turn(*us[-1])
            weigh(*us[-2])
            weigh(*us[-1])

        @block.scalar
        def _(act):
            def exponentials(blk, u, n):
                act.wait_ge(negmax_ready, n + 1)
                wait(act, probs_turned, n - 1)
                for half in range(2):
                    for pr in range(2):
                        h = head(u, half, pr)
                        ins = nc.scalar.activation(
                            prob[u][:, half, pr, blk.c0 * P:2 * P], psS[u][:, half, pr, blk.c0 * P:2 * P], ACT.Exp,
                            bias=ob[blk.j][:, W + h:W + h + 1], scale=SCALE,
                            accum_out=ob[blk.j][:, W + H + h:W + H + h + 1])
                ins.then_inc(exp_done, 1)

            def keep_half(blk, u, n):
                act.wait_ge(probs_turned, n + 1)
                wait(act, weighted, n - 1)
                nc.scalar.copy(probT[u][:, 1, :, blk.c0:2, :], psT[:, 1, :, blk.c0:2, :]).then_inc(kept_by_act, 1)

            def store(blk):
                act.wait_ge(o_ready, blk.n + 1)
                act.wait_ge(exp_done, 2 * blk.n + 2)
                act.dma_start(scratch["o"][blk.branch, blk.tokens, :], ob[blk.j][:]
                              ).then_inc(o_out[blk.j], 16)

            def body(group, before):
                us, old = units(before + group), 2 * len(before)
                for s in range(old, len(us)):
                    exponentials(*us[s])
                    if s >= 1:
                        keep_half(*us[s - 1])
                    if s >= 4 and s % 2 == 0:
                        store(us[s - 4][0])
            before = over_groups(act, body)
            keep_half(*units(before)[-1])
            for blk in before:
                store(blk)
            for r in range(4):
                act.wait_ge(o_out[r], 16 * 3 * T // 4)

        @block.vector
        def _(dve):
            v = nc.vector

            def maxima(blk, u, n):
                dve.wait_ge(scores_ready, n + 1)
                wait(dve, negmax_ready, n - 1)
                v.tensor_reduce(top[u][:], psS[u][:, :, :, blk.c0 * P:2 * P], AX.X, ALU.max).then_inc(top_ready, 1)
                dve.wait_ge(top_ready, n + 1)
                if u == 0:
                    wait(dve, o_out[blk.j], 16 * round_of(blk))
                v.tensor_scalar(ob[blk.j][:, W + 4 * u:W + 4 * u + 4].rearrange("p (a b) -> p b a", b=2),
                                top[u][:], -SCALE, None, ALU.mult).then_inc(negmax_ready, 1)

            def keep_half(blk, u, n):
                dve.wait_ge(probs_turned, n + 1)
                wait(dve, weighted, n - 1)
                v.tensor_copy(probT[u][:, 0, :, blk.c0:2, :], psT[:, 0, :, blk.c0:2, :]).then_inc(kept_by_dve, 1)

            def outputs(blk):
                dve.wait_ge(weighted, 2 * blk.n + 2)
                v.tensor_copy(ob[blk.j][:, 0:W], psO[blk.j % 2][:]).then_inc(o_ready, 1)

            def body(group, before):
                us, old = units(before + group), 2 * len(before)
                for s in range(old, len(us)):
                    maxima(*us[s])
                    if s >= 1:
                        keep_half(*us[s - 1])
                    if s >= 3 and s % 2 == 1:
                        outputs(us[s - 2][0])

            dve.wait_ge(mask_in, 16)
            v.tensor_copy(identb[:], keep["ident"][:]).then_inc(mask_ready, 1)
            v.tensor_copy(mask[:], mask_in_f32[:]).then_inc(mask_ready, 1)
            before = over_groups(dve, body)
            keep_half(*units(before)[-1])
            outputs(before[-1])


def mixing_stage(nc, io, scratch, keep):
    with ExitStack() as ctx:
        sb = lambda s, shape, dt=F32: ctx.enter_context(nc.sbuf_tensor(f"mi_{s}", shape, dt))
        ps = lambda s, shape: ctx.enter_context(nc.psum_tensor(f"mi_ps_{s}", shape, F32))
        sem = stage_semaphores(nc, ctx, "mi")
        NB = len(DILATIONS)
        mixed = [sb(f"mixed{p}", [P, D]) for p in range(2)]
        f = Front(nc, ctx, sem, "mi", keep, io["mix_g"], io["w_out"], (0, W), rows=mixed)
        rows_o = [sb(f"rows{p}", [P, NB, OROW]) for p in range(2)]
        xt = [sb(f"x{p}", [P, D]) for p in range(2)]
        low, total, inverse = sb("low", [P, H]), sb("total", [P, H]), sb("inverse", [P, H])
        diff, weight, share = sb("diff", [P, NB, H]), sb("weight", [P, NB, H]), sb("share", [P, NB, H])
        coef = [sb(f"coef{p}", [P, NB, H]) for p in range(2)]
        scaled = sb("scaled", [P, NB, H, DH])
        partial = sb("partial", [P, H, DH])
        bo = [sb(f"bo{p}", [P, H, DH]) for p in range(2)]
        squares = sb("squares", [P, D])
        bst, hst = sb("bst", [P, 2, 2]), sb("hst", [P, 2, 2])
        work = sb("work", [P, ROOT_WORK, 1])
        h = [sb(f"h{p}", [P, D]) for p in range(2)]
        hs = [sb(f"hs{p}", [P, D]) for p in range(2)]
        hT = sb("hT", [P, KD, P])
        g2, wr, br = sb("g2", [P, D]), sb("wr", [P, KD, E]), sb("br", [P, E])
        psH = [ps(f"h{n}", [P, W]) for n in range(2)]
        psT = ps("hT", [P, KD, P])
        psR = ps("r", [P, E])

        o_in, a_in, x_in, h_out, hs_out = ([sem(f"{s}{p}") for p in range(2)]
                                           for s in ("o_in", "a_in", "x_in", "h_out", "hs_out"))
        g2_in, wr_in, br_in = sem("g2_in"), sem("wr_in"), sem("br_in")
        low_ready, diff_ready, weight_ready = sem("low_ready"), sem("diff_ready"), sem("weight_ready")
        coef_steps, coef_ready = sem("coef_steps"), sem("coef_ready")
        scaled_ready, partial_ready, bo_ready = sem("scaled_ready"), sem("partial_ready"), sem("bo_ready")
        b_squares, b_root, b_scale = sem("b_squares"), sem("b_root"), sem("b_scale")
        half_done = sem("half_done")
        h_halves, h_squares, h_root, h_scale = sem("h_halves"), sem("h_squares"), sem("h_root"), sem("h_scale")
        hs_scaled, hs_ready, h_turned, hT_ready, routed = sem("hs_scaled"), sem("hs_ready"), sem("h_turned"), sem("hT_ready"), sem("routed")
        logits_ready = sem("logits_ready")
        block = ctx.enter_context(nc.Block())

        @block.sync
        def _(sp):
            def load(tile):
                p = tile.p
                wait(sp, scaled_ready, tile.t - 1)
                sp.dma_start(rows_o[p][:], scratch["o"][:, tile.rows, :].rearrange("b p w -> p b w")
                             ).then_inc(o_in[p], 16)
                wait(sp, f.turned, tile.t - 1)
                sp.dma_start(mixed[p][:, 0:W], scratch["a"][tile.rows, :]).then_inc(a_in[p], 16)

            def load_x(tile):
                wait(sp, h_halves, 2 * tile.t - 2)
                sp.dma_start(xt[tile.p][:], io["x"][tile.rows, :]).then_inc(x_in[tile.p], 16)

            load(Tile(0, 0))
            load(Tile(0, 1))
            f.load_gains(sp)
            f.load_weights(sp)
            sp.dma_start(g2[:], io["norm2_g"].to_broadcast([P, D])).then_inc(g2_in, 16)
            sp.dma_start(wr[:], io["w_router"]).then_inc(wr_in, 16)
            sp.dma_start(br[:], io["b_router"].to_broadcast([P, E])).then_inc(br_in, 16)
            load_x(Tile(0, 0))

            def load_pair(i):
                for p in range(2):
                    load(Tile(i, p))
                    load_x(Tile(i, p).at(-1))

            load_pair(1)
            with sp.Fori(2, T // 2) as i:
                load_pair(i)
            load_x(Tile(T // 2 - 1, 1))

        @block.gpsimd
        def _(pool):
            def sum_branches(tile):
                p, t, g = tile.p, tile.t, nc.gpsimd
                pool.wait_ge(coef_ready, t + 1)
                wait(pool, bo_ready, t)
                g.tensor_tensor(scaled[:], rows_o[p][:, :, 0:W].rearrange("p b (h d) -> p b h d", h=H),
                                coef[p][:].unsqueeze(3).to_broadcast([P, NB, H, DH]), ALU.mult
                                ).then_inc(scaled_ready, 1)
                pool.wait_ge(scaled_ready, t + 1)
                g.tensor_tensor(partial[:], scaled[:, 0], scaled[:, 1], ALU.add).then_inc(partial_ready, 1)
                pool.wait_ge(partial_ready, t + 1)
                wait(pool, f.xn_ready, t - 1)
                g.tensor_tensor(bo[p][:], partial[:], scaled[:, 2], ALU.add).then_inc(bo_ready, 1)

            def gain_hidden(tile):
                pool.wait_ge(hs_scaled, tile.t + 1)
                nc.gpsimd.tensor_tensor(hs[tile.p][:], hs[tile.p][:], g2[:], ALU.mult).then_inc(hs_ready, 1)

            def body(tile):
                if tile.has(3):
                    sum_branches(tile.at(3))
                gain_hidden(tile)

            for tile in (Tile(0, 0), Tile(0, 1), Tile(1, 0)):
                sum_branches(tile)
            pool.wait_ge(g2_in, 16)
            over_tiles(pool, body, 3)

        @block.tensor
        def _(pe):
            def turn_mixed(tile):
                pe.wait_ge(a_in[tile.p], 16 * tile.i + 16)
                f.turn_x(pe, tile)

            def turn_hidden(tile):
                pe.wait_ge(hs_ready, tile.t + 1)
                wait(pe, hT_ready, tile.t)
                for k in range(KD):
                    ins = pe.transpose(psT[:, k, :], hs[tile.p][:, k * P:(k + 1) * P], keep["ident"][:])
                ins.then_inc(h_turned, 1)

            def route(tile):
                pe.wait_ge(hT_ready, tile.t + 1)
                wait(pe, logits_ready, tile.t)
                for k in range(KD):
                    ins = pe.matmul(psR[:], hT[:, k, :], wr[:, k, :], start=(k == 0), stop=(k == KD - 1))
                ins.then_inc(routed, 1)

            def body(tile):
                if tile.has(1):
                    turn_mixed(tile.at(1))
                pe.wait_ge(f.lo_ready, tile.t + 1)
                for n in range(2):
                    wait(pe, h_halves, 2 * tile.t + n - 1)
                    ins = f.gemm(pe, tile, n, psH[n][:])
                    ins.then_inc(f.gemm_done if n else half_done, 1)
                if tile.has(-2):
                    route(tile.at(-2))
                if tile.has(-1):
                    turn_hidden(tile.at(-1))

            turn_mixed(Tile(0, 0))
            pe.wait_ge(wr_in, 16)
            over_tiles(pe, body, 3, peeled=2)
            route(Tile(T // 2 - 1, 0))
            turn_hidden(Tile(T // 2 - 1, 1))
            route(Tile(T // 2 - 1, 1))

        @block.scalar
        def _(act):
            def weights(tile):
                act.wait_ge(diff_ready, tile.t + 1)
                wait(act, coef_ready, tile.t)
                nc.scalar.activation(weight[:], diff[:], ACT.Exp).then_inc(weight_ready, 1)

            def scale_b(tile):
                act.wait_ge(b_scale, tile.t + 1)
                wait(act, f.turned, tile.t - 1)
                nc.scalar.mul(mixed[tile.p][:, W:D], bo[tile.p][:].rearrange("p h d -> p (h d)"),
                              bst[:, tile.p, 1:2]).then_inc(f.xn_ready, 1)

            def scale_hidden(tile):
                p = tile.p
                act.wait_ge(h_scale, tile.t + 1)
                wait(act, hs_out[p], 16 * tile.i)
                wait(act, h_turned, tile.t - 1)
                nc.scalar.mul(hs[p][:], h[p][:], hst[:, p, 1:2]).then_inc(hs_scaled, 1)
                act.dma_start(scratch["h"][tile.rows, :], h[p][:]).then_inc(h_out[p], 16)

            def keep_hidden(tile):
                act.wait_ge(h_turned, tile.t + 1)
                wait(act, routed, tile.t)
                nc.scalar.copy(hT[:], psT[:]).then_inc(hT_ready, 1)
                act.wait_ge(hs_ready, tile.t + 1)
                act.dma_start(scratch["hn"][tile.rows, :], hs[tile.p][:]).then_inc(hs_out[tile.p], 16)

            def body(tile):
                if tile.has(1):
                    f.hi_x(act, tile.at(1))
                if tile.has(3):
                    weights(tile.at(3))
                if tile.has(-1):
                    scale_hidden(tile.at(-1))
                if tile.has(2):
                    scale_b(tile.at(2))
                if tile.has(-1):
                    keep_hidden(tile.at(-1))

            act.wait_ge(f.g_in, 16)
            weights(Tile(0, 0))
            weights(Tile(0, 1))
            f.weights_hi(act, 0)
            scale_b(Tile(0, 0))
            f.hi_x(act, Tile(0, 0))
            f.weights_hi(act, 1)
            scale_b(Tile(0, 1))
            weights(Tile(1, 0))
            over_tiles(act, body, 3, peeled=2)
            scale_hidden(Tile(T // 2 - 1, 1))
            keep_hidden(Tile(T // 2 - 1, 1))
            for p in range(2):
                act.wait_ge(h_out[p], 16 * (T // 2))
                act.wait_ge(hs_out[p], 16 * (T // 2))

        @block.vector
        def _(dve):
            v = nc.vector

            def distances(tile):
                p, t = tile.p, tile.t
                negmax = rows_o[p][:, :, W:W + H]
                dve.wait_ge(o_in[p], 16 * tile.i + 16)
                wait(dve, diff_ready, t)
                v.tensor_reduce(low[:], negmax.rearrange("p b h -> p h b"), AX.X, ALU.min).then_inc(low_ready, 1)
                dve.wait_ge(low_ready, t + 1)
                wait(dve, weight_ready, t)
                v.tensor_tensor(diff[:], low[:].unsqueeze(1).to_broadcast([P, NB, H]), negmax, ALU.subtract
                                ).then_inc(diff_ready, 1)

            def coefficients(tile):
                p, t = tile.p, tile.t
                c = Chain(dve, coef_steps, 3 * t)
                dve.wait_ge(weight_ready, t + 1)
                c.then(v.tensor_tensor(share[:], weight[:], rows_o[p][:, :, W + H:OROW], ALU.mult))
                c.then(v.reduce_sum(total[:], share[:].rearrange("p b h -> p h b"), AX.X))
                c.then(v.reciprocal(inverse[:], total[:]))
                wait(dve, scaled_ready, t - 1)
                v.tensor_tensor(coef[p][:], weight[:], inverse[:].unsqueeze(1).to_broadcast([P, NB, H]), ALU.mult
                                ).then_inc(coef_ready, 1)

            def norm_b(tile):
                p, t = tile.p, tile.t
                flat = bo[p][:].rearrange("p h d -> p (h d)")
                dve.wait_ge(bo_ready, t + 1)
                wait(dve, f.xn_ready, t - 1)
                v.tensor_tensor_reduce(squares[:, 0:W], flat, flat, 1.0, 0.0, ALU.mult, ALU.add, bst[:, p, 0:1]
                                       ).then_inc(b_squares, 1)
                dve.wait_ge(b_squares, t + 1)
                inverse_root(nc, Chain(dve, b_root, ROOT_STEPS * t), 1.0 / W, bst[:, p, 0:1], work[:],
                             bst[:, p, 1:2]).then_inc(b_scale, 1)
                dve.wait_ge(b_scale, t + 1)

            def residual(tile):
                p, t = tile.p, tile.t
                dve.wait_ge(x_in[p], 16 * tile.i + 16)
                wait(dve, h_out[p], 16 * tile.i)
                for n in range(2):
                    if n:
                        dve.wait_ge(f.gemm_done, t + 1)
                    else:
                        dve.wait_ge(half_done, t + 1)
                    cols = slice(n * W, n * W + W)
                    v.tensor_tensor(h[p][:, cols], psH[n][:], xt[p][:, cols], ALU.add).then_inc(h_halves, 1)
                dve.wait_ge(h_halves, 2 * t + 2)
                v.tensor_tensor_reduce(squares[:], h[p][:], h[p][:], 1.0, 0.0, ALU.mult, ALU.add, hst[:, p, 0:1]
                                       ).then_inc(h_squares, 1)
                dve.wait_ge(h_squares, t + 1)
                inverse_root(nc, Chain(dve, h_root, ROOT_STEPS * t), 1.0 / D, hst[:, p, 0:1], work[:],
                             hst[:, p, 1:2]).then_inc(h_scale, 1)
                dve.wait_ge(h_scale, t + 1)

            def keep_logits(tile):
                dve.wait_ge(routed, tile.t + 1)
                v.tensor_tensor(keep["logits"][:, bass.ds(tile.t, 1), :], psR[:].unsqueeze(1),
                                br[:].unsqueeze(1), ALU.add).then_inc(logits_ready, 1)

            def body(tile):
                if tile.has(1):
                    f.lo_x(dve, tile.at(1))
                if tile.has(3):
                    distances(tile.at(3))
                if tile.has(2):
                    norm_b(tile.at(2))
                if tile.has(3):
                    coefficients(tile.at(3))
                residual(tile)
                if tile.has(-2):
                    keep_logits(tile.at(-2))

            dve.wait_ge(f.g_in, 16)
            for tile in (Tile(0, 0), Tile(0, 1)):
                distances(tile)
                coefficients(tile)
            norm_b(Tile(0, 0))
            f.weights_lo(dve, 0)
            f.lo_x(dve, Tile(0, 0))
            f.weights_lo(dve, 1)
            norm_b(Tile(0, 1))
            distances(Tile(1, 0))
            coefficients(Tile(1, 0))
            dve.wait_ge(br_in, 16)
            over_tiles(dve, body, 3)
            keep_logits(Tile(T // 2 - 1, 0))
            keep_logits(Tile(T // 2 - 1, 1))


PE_WIDTHS = (*range(160, 385, 32), 448, SLOT)
TILE_WIDTHS = (256, 384, SLOT)
EXPERT, PE_CLASS, TILE_CLASS, USED = range(4)
ENTRY = 4


def routing_stage(nc, io, scratch, keep):
    with ExitStack() as ctx:
        sb = lambda s, shape, dt=F32: ctx.enter_context(nc.sbuf_tensor(f"rt_{s}", shape, dt))
        sem = stage_semaphores(nc, ctx, "rt")
        token_mark, numbers = sb("token_mark", [P, T]), sb("numbers", [P, COLS])
        place, place_hi, place_lo = (sb(s, [P, T, TOPK], U32) for s in ("place", "place_hi", "place_lo"))
        spot_hi, spot_lo = sb("spot_hi", [P, T, TOPK]), sb("spot_lo", [P, T, TOPK])
        marks, spots = sb("marks", [P, T, TOPK, P], F32R), sb("spots", [P, T, TOPK, COLS], F32R)
        blank_i, blank = sb("blank_i", [P, COLS], U32), sb("blank", [P, COLS])
        mark, listed, picks = sb("mark", [P, COLS]), sb("listed", [P, COLS]), sb("picks", [P, COLS])
        choice, target = sb("choice", [P, TOPK, COLS]), sb("target", [P, COLS])
        expert, slot, before, ones = sb("expert", [P, E]), sb("slot", [P, 1]), sb("before", [P, P]), sb("ones", [P, P])
        topv, topi, chosen = sb("topv", [P, T, 8]), sb("topi", [P, T, 8], U32), sb("chosen", [P, T, TOPK])
        shifted, power, power_sum = sb("shifted", [P, T, TOPK]), sb("power", [P, T, TOPK]), sb("power_sum", [P, T])
        power_inv = sb("power_inv", [P, T])
        hot = sb("hot", [P, TOPK, T, E])
        picked = sb("picked", [P, T, E])
        weighted = sb("weighted", [P, T, E])
        tile_counts, running = sb("tile_counts", [P, E, T]), sb("running", [P, E, T])
        restart = sb("restart", [P, E, T])
        slots_of, slot_end, slot_first = sb("slots_of", [P, E]), sb("slot_end", [P, E]), sb("slot_first", [P, E])
        row_first, row_end = sb("row_first", [P, E]), sb("row_end", [P, E])
        position = sb("position", [P, T, E])
        places = sb("places", [P, T, TOPK])
        ended, begun, left = sb("ended", [P, E]), sb("begun", [P, E]), sb("left", [P, E])
        tokens_of, entry, entry_i = sb("tokens_of", [P, 2]), sb("entry", [P, ENTRY]), sb("entry_i", [P, ENTRY], I32)
        slot_rows = sb("slot_rows", [P, 1])
        psRank = ctx.enter_context(nc.psum_tensor("rt_ps_rank", [P, T, E], F32))
        psList = ctx.enter_context(nc.psum_tensor("rt_ps_list", [P, TOPK, LIST_STRIDE], F32))
        psCount = ctx.enter_context(nc.psum_tensor("rt_ps_count", [P, T, E], F32))

        consts_in = [sem(f"in_{n}") for n in range(5)]
        blank_ready, spots_known, pool_marks, spots_ready = (
            sem(s) for s in ("blank_ready", "spots_known", "pool_marks", "spots_ready"))
        summed = sem("summed")
        steps = sem("steps")
        max_ready, exp_ready, picked_ready, ranked = sem("max_ready"), sem("exp_ready"), sem("picked_ready"), sem("ranked")
        table_ready, table_out, table_back = sem("table_ready"), sem("table_out"), sem("table_back")
        block = ctx.enter_context(nc.Block())

        POOL_TILES = range(3, T, 4)

        def mark_rows(eng, t):
            for k in range(TOPK):
                ins = eng.tensor_scalar(marks[:, t, k, :], numbers[:, 0:P], spot_lo[:, t, k:k + 1],
                                        token_mark[:, t:t + 1], ALU.is_equal, ALU.mult)
            return ins

        @block.sync
        def _(sp):
            for n, (dst, src) in enumerate(((token_mark[:], io["token_mark"]), (expert[:], io["expert"].to_broadcast([P, E])),
                                            (slot[:], io["slot"]), (before[:], io["before"]),
                                            (numbers[:], io["column"].to_broadcast([P, COLS])))):
                sp.dma_start(dst, src).then_inc(consts_in[n], 16)
            sp.wait_ge(table_ready, 1)
            sp.dma_start(scratch["table"], entry_i[0:NSLOTS + 1, :]).then_inc(table_out, 16)
            sp.wait_ge(table_out, 16)
            sp.dma_start(keep["table"][:], scratch["table"].rearrange("s w -> (s w)").rearrange("(a n) -> a n", a=1)
                         ).then_inc(table_back, 16)
            sp.wait_ge(table_back, 16)

        @block.gpsimd
        def _(pool):
            nc.gpsimd.iota(blank_i[:], pattern=[[2 * P, COLS]], base=2 * S * TOPK, channel_multiplier=2
                           ).then_inc(blank_ready, 1)
            pool.wait_ge(consts_in[0], 16)
            pool.wait_ge(consts_in[4], 16)
            pool.wait_ge(spots_known, 2)
            for t in POOL_TILES:
                mark_rows(nc.gpsimd, t).then_inc(pool_marks, 1)

        @block.tensor
        def _(pe):
            pe.wait_ge(consts_in[3], 16)
            pe.wait_ge(picked_ready, 1)
            flat = picked[:].rearrange("p t e -> p (t e)")
            pe.matmul(psCount[:].rearrange("p t e -> p (t e)"), ones[:], flat, start=True, stop=True)
            pe.matmul(psRank[:].rearrange("p t e -> p (t e)"), before[:], flat, start=True, stop=True
                      ).then_inc(ranked, 1)
            for t in range(T):
                pe.wait_ge(spots_ready, t + 1)
                if t in POOL_TILES:
                    pe.wait_ge(pool_marks, POOL_TILES.index(t) + 1)
                for k in range(TOPK):
                    ins = pe.matmul(psList[:, k, 0:COLS], marks[:, t, k, :], spots[:, t, k, :],
                                    start=(t == 0), stop=(t == T - 1))
            ins.then_inc(summed, 1)

        @block.scalar
        def _(act):
            act.wait_ge(max_ready, 1)
            nc.scalar.activation(power[:], shifted[:], ACT.Exp).then_inc(exp_ready, 1)

        @block.vector
        def _(dve):
            v = nc.vector
            c = Chain(dve, steps, 0)
            wide = lambda x: x.unsqueeze(1).to_broadcast([P, T, E])
            v.memset(ones[:], 1.0)
            v.memset(restart[:], 1.0)
            for t in range(T):
                last = v.max(topv[:, t, :], keep["logits"][:, t, :])
            c.then(last)
            v.memset(restart[:, :, 0:1], 0.0)
            for t in range(T):
                v.max_index(topi[:, t, :], topv[:, t, :], keep["logits"][:, t, :])
            c.then(v.tensor_tensor(shifted[:], topv[:, :, 0:TOPK], topv[:, :, 0:1].to_broadcast([P, T, TOPK]),
                                   ALU.subtract))
            v.tensor_copy(chosen[:], topi[:, :, 0:TOPK]).then_inc(max_ready, 1)
            dve.wait_ge(max_ready, 1)
            dve.wait_ge(consts_in[1], 16)
            for k in range(TOPK):
                last = v.tensor_tensor(hot[:, k], wide(expert[:]), chosen[:, :, k:k + 1].to_broadcast([P, T, E]),
                                       ALU.is_equal)
            c.then(last)
            v.tensor_tensor(position[:], hot[:, 0], hot[:, 1], ALU.add)
            c.then(v.tensor_tensor(weighted[:], hot[:, 2], hot[:, 3], ALU.add))
            v.tensor_tensor(picked[:], position[:], weighted[:], ALU.add).then_inc(picked_ready, 1)
            dve.wait_ge(picked_ready, 1)
            dve.wait_ge(ranked, 1)
            c.then(v.tensor_copy(tile_counts[:], psCount[:].rearrange("p t e -> p e t")))
            c.then(v.tensor_tensor_scan(running[:].rearrange("p e t -> p (e t)"), restart[:].rearrange("p e t -> p (e t)"),
                                        tile_counts[:].rearrange("p e t -> p (e t)"), 0.0, ALU.mult, ALU.add))
            counts = running[:, :, T - 1]
            c.then(v.tensor_scalar(slots_of[:], counts, 0.0, None, ALU.is_gt))
            for j in range(1, S // SLOT):
                c.then(v.scalar_tensor_tensor(slots_of[:], counts, float(SLOT * j), slots_of[:], ALU.is_gt, ALU.add))
            c.then(v.tensor_tensor_scan(slot_end[:], ones[:, 0:E], slots_of[:], 0.0, ALU.mult, ALU.add))
            c.then(v.tensor_tensor(slot_first[:], slot_end[:], slots_of[:], ALU.subtract))
            c.then(v.tensor_scalar(row_first[:], slot_first[:], float(SLOT), None, ALU.mult))
            c.then(v.tensor_tensor(row_end[:], row_first[:], counts, ALU.add))
            c.then(v.tensor_tensor(running[:], running[:], tile_counts[:], ALU.subtract))
            c.then(v.tensor_tensor(position[:], psRank[:], running[:].rearrange("p e t -> p t e"), ALU.add))
            c.then(v.tensor_tensor(position[:], position[:], wide(row_first[:]), ALU.add))
            for k in range(TOPK):
                c.then(v.tensor_tensor(weighted[:], hot[:, k], position[:], ALU.mult))
                c.then(v.reduce_sum(places[:, :, k], weighted[:], AX.X))
            c.then(v.tensor_copy(place[:], places[:]))
            v.tensor_scalar(place_hi[:], place[:], P_BITS, None, ALU.logical_shift_right)
            c.then(v.tensor_scalar(place_lo[:], place[:], P - 1, None, ALU.bitwise_and))
            v.tensor_copy(spot_lo[:], place_lo[:]).then_inc(spots_known, 1)
            v.tensor_copy(spot_hi[:], place_hi[:]).then_inc(spots_known, 1)
            dve.wait_ge(spots_known, 2)
            dve.wait_ge(consts_in[4], 16)

            dve.wait_ge(consts_in[0], 16)

            def one_hot(tiles):
                for t in tiles:
                    if t not in POOL_TILES:
                        mark_rows(v, t)
                    v.tensor_tensor(spots[:, t], numbers[:].unsqueeze(1).to_broadcast([P, TOPK, COLS]),
                                    spot_hi[:, t, :].unsqueeze(2).to_broadcast([P, TOPK, COLS]), ALU.is_equal
                                    ).then_inc(spots_ready, 1)

            one_hot(range(TOPK))
            dve.wait_ge(consts_in[2], 16)
            c.then(v.tensor_scalar(slot_rows[:], slot[:], float(SLOT), None, ALU.mult))
            v.tensor_scalar(ended[:], slot_end[:], slot[:, 0:1], None, ALU.is_le)
            v.tensor_scalar(begun[:], slot_first[:], slot[:, 0:1], None, ALU.is_le)
            c.then(v.tensor_scalar(left[:], row_end[:], slot_rows[:, 0:1], None, ALU.subtract))
            c.then(v.tensor_tensor(begun[:], begun[:], ended[:], ALU.subtract))
            c.then(v.tensor_tensor(left[:], left[:], begun[:], ALU.mult))
            v.reduce_sum(tokens_of[:, 0:1], ended[:], AX.X)
            c.then(v.reduce_sum(tokens_of[:, 1:2], left[:], AX.X))
            v.tensor_scalar(entry[:, EXPERT:EXPERT + 1], tokens_of[:, 0:1], float(E - 1), None, ALU.min)
            v.tensor_copy(entry[:, USED:USED + 1], slot_end[:, E - 1:E])
            for column, widths in ((PE_CLASS, PE_WIDTHS), (TILE_CLASS, TILE_WIDTHS)):
                kind = entry[:, column:column + 1]
                c.then(v.tensor_scalar(kind, tokens_of[:, 1:2], 0.0, None, ALU.is_gt))
                for w in widths[:-1]:
                    c.then(v.scalar_tensor_tensor(kind, tokens_of[:, 1:2], float(w), kind, ALU.is_gt, ALU.add))
            v.tensor_copy(entry_i[:], entry[:]).then_inc(table_ready, 1)
            one_hot(range(TOPK, T))
            dve.wait_ge(table_ready, 1)
            dve.wait_ge(exp_ready, 1)
            c.then(v.reduce_sum(power_sum[:], power[:], AX.X))
            c.then(v.reciprocal(power_inv[:], power_sum[:]))
            c.then(v.tensor_tensor(keep["gates"][:], power[:], power_inv[:].unsqueeze(2).to_broadcast([P, T, TOPK]),
                                   ALU.mult))
            c.then(v.tensor_tensor(keep["spread"][:], hot[:, 0], keep["gates"][:, :, 0:1].to_broadcast([P, T, E]),
                                   ALU.mult))
            for k in range(1, TOPK):
                c.then(v.tensor_tensor(weighted[:], hot[:, k], keep["gates"][:, :, k:k + 1].to_broadcast([P, T, E]),
                                       ALU.mult))
                c.then(v.tensor_tensor(keep["spread"][:], keep["spread"][:], weighted[:], ALU.add))
            dve.wait_ge(blank_ready, 1)
            c.then(v.tensor_copy(blank[:], blank_i[:]))
            dve.wait_ge(summed, 1)
            v.reduce_sum(mark[:], psList[:, :, 0:COLS].rearrange("p k c -> p c k"), AX.X)
            for k in range(1, TOPK):
                last = v.tensor_scalar(choice[:, k, :], psList[:, k, 0:COLS], 0.0, 2.0 * k, ALU.is_gt, ALU.mult)
            c.then(last)
            v.tensor_scalar(listed[:], mark[:], 0.0, None, ALU.is_gt)
            v.tensor_scalar(keep["tokens"][:], mark[:], -1.0, 0.0, ALU.add, ALU.max)
            v.tensor_scalar(target[:], mark[:], 2.0 * TOPK, -2.0 * TOPK, ALU.mult, ALU.add)
            c.then(v.tensor_tensor(picks[:], choice[:, 1, :], choice[:, 2, :], ALU.add))
            c.then(v.tensor_tensor(picks[:], picks[:], choice[:, 3, :], ALU.add))
            c.then(v.tensor_tensor(target[:], target[:], picks[:], ALU.add))
            c.then(v.tensor_tensor(target[:], target[:], blank[:], ALU.subtract))
            c.then(v.tensor_tensor(target[:], target[:], listed[:], ALU.mult))
            c.then(v.tensor_tensor(target[:], target[:], blank[:], ALU.add))
            v.tensor_copy(keep["targets"][:], target[:])


def tile_count(width):
    return -(-width // P)


def table_entry(eng, keep, s, column, most):
    return eng.value_load(keep["table"][0:1, bass.ds(ENTRY * s + column, 1)], min_val=0, max_val=most)


def by_class(eng, kind, widths, body, first=1):
    if len(widths) <= 3:
        for c, width in enumerate(widths):
            with eng.If(kind == first + c):
                body(width)
    else:
        half = len(widths) // 2
        with eng.If(kind < first + half):
            by_class(eng, kind, widths[:half], body, first)
        with eng.If(kind >= first + half):
            by_class(eng, kind, widths[half:], body, first + half)


def over_slots(eng, keep, *steps):
    used = table_entry(eng, keep, 0, USED, NSLOTS)
    with eng.Fori(0, NSLOTS) as s:
        with eng.If(s < used):
            kinds = {}
            for ahead, column, widths, _ in steps:
                if (ahead, column) not in kinds:
                    kinds[ahead, column] = table_entry(eng, keep, s + ahead, column, len(widths))
            for ahead, column, widths, body in steps:
                by_class(eng, kinds[ahead, column], widths, lambda width: body(s, width))


def for_first_slot(eng, keep, body):
    kind = table_entry(eng, keep, 0, TILE_CLASS, len(TILE_WIDTHS))
    by_class(eng, kind, TILE_WIDTHS, lambda width: body(0, width))


def experts_stage(nc, io, scratch, keep):
    PIECES, BUFFERS = 12, 4
    PIECE = KD * 2 * P
    FB = 2
    NF = FF // P
    FH = NF // 2
    HALF = D // 2
    BANKS = 4
    TURN = 10
    USES = 3 * KD
    OPEN, OPEN_DMA = 1, 16
    with ExitStack() as ctx:
        sb = lambda s, shape, dt=F32: ctx.enter_context(nc.sbuf_tensor(f"ex_{s}", shape, dt))
        ps = lambda s, shape: ctx.enter_context(nc.psum_tensor(f"ex_ps_{s}", shape, F32))
        sem = stage_semaphores(nc, ctx, "ex")
        raw = [sb(f"raw{r}", [P, PIECE]) for r in range(BUFFERS)]
        w = [sb(f"w{r}", [P, 2, PIECE], F32R) for r in range(BUFFERS)]
        idx, dest = sb("idx", [P, ST], U32), sb("dest", [P, ST, 2], U32)
        xg = sb("xg", [P, ST, D])
        xT = sb("xT", [P, 2, KD, SLOT], F32R)
        gate = sb("gate", [P, 2 * FB, SLOT])
        sig = [sb(f"sig{r}", [P, SLOT]) for r in range(2)]
        up = [sb(f"up{r}", [P, SLOT]) for r in range(2)]
        actT = sb("actT", [P, 2, NF, SLOT], F32R)
        y = sb("y", [P, ST, HALF])
        bgu, bias = sb("bgu", [P, E, 2 * FF // P]), sb("bias", [P, 2 * FF // P])
        ring = [ps(f"ring{b}", [P, SLOT]) for b in range(BANKS)]
        psY = [ps(f"y{j}", [P, HALF]) for j in range(ST)]

        raw_in = [sem(f"raw_in{r}") for r in range(BUFFERS)]
        idx_ready, x_in = sem("idx_ready"), sem("x_in")
        w_hi, w_lo = sem("w_hi"), sem("w_lo")
        banks_zeroed = sem("banks_zeroed")
        bank_full, bank_free = sem("bank_full"), sem("bank_free")
        x_hi = sem("x_hi")
        bias_ready = sem("bias_ready")
        sig_ready, swish_ready = sem("sig_ready"), sem("swish_ready")
        up_ready, act_ready = sem("up_ready"), sem("act_ready")
        act_hi, act_lo = sem("act_hi"), sem("act_lo")
        y_full, y_free = sem("y_full"), sem("y_free")
        y_out = sem("y_out")
        dest_ready = sem("dest_ready")
        gather_go, scatter_go, all_stored, fetched = (sem(s) for s in ("gather_go", "scatter_go", "all_stored", "fetched"))
        block = ctx.enter_context(nc.Block())

        def piece_done(s, q):
            if q < 8:
                return bank_full, KD + USES * s + FB * (q + 1)
            return y_full, OPEN + 4 * ST * s + ST * (q - 7)

        def per_bank(width):
            return SLOT // width

        def turned(b, width):
            n = per_bank(width)
            return ring[b % BANKS][:, 0:n * width].rearrange("p (k c) -> p k c", k=n)

        @block.sync
        def _(sp):
            def load(e, q):
                if q < 8:
                    c0 = (q % 2) * FF + (q // 2) * FB * P
                    src = io["w_gate_up"][bass.ds(e, 1), :, c0:c0 + FB * P]
                else:
                    dh, fh = divmod(q - 8, 2)
                    src = io["w_down"][bass.ds(e, 1), fh * FH * P:(fh + 1) * FH * P, dh * HALF:(dh + 1) * HALF]
                src = src.rearrange("o (k p) n -> p (o k) n", p=P)
                sp.dma_start(raw[q % BUFFERS][:].rearrange("p (k n) -> p k n", n=src.shape[2]), src
                             ).then_inc(raw_in[q % BUFFERS], 16)

            first = table_entry(sp, keep, 0, EXPERT, E - 1)
            for q in range(BUFFERS):
                load(first, q)
            used = table_entry(sp, keep, 0, USED, NSLOTS)
            with sp.Fori(0, NSLOTS) as s:
                with sp.If(s < used):
                    e, e_next = (table_entry(sp, keep, s + d, EXPERT, E - 1) for d in range(2))
                    for q in range(PIECES):
                        sp.wait_ge(w_lo, OPEN + PIECES * s + q + 1)
                        load(e if q + BUFFERS < PIECES else e_next, (q + BUFFERS) % PIECES)
            sp.wait_ge(raw_in[BUFFERS - 1], used * (16 * PIECES // BUFFERS) + 16)
            sp.sem_inc(fetched, 1)

        @block.gpsimd
        def _(pool):
            g = nc.gpsimd

            def gather(s, width):
                tiles = tile_count(width)
                pool.wait_ge(idx_ready, s + 1)
                pool.sem_inc(gather_go, 1)
                for j in range(tiles):
                    g.indirect_dma_start(
                        out=xg[:, j, :], out_offset=None, in_=scratch["hn"],
                        in_offset=bass.IndirectOffsetOnAxis(ap=idx[:, j:j + 1], axis=0)
                        ).then_inc(x_in, 16 if j < tiles - 1 else 16 * (ST - tiles + 1))

            def scatter(s, half, tiles):
                pool.wait_ge(y_free, OPEN + 2 * ST * s + ST * half + ST)
                if half == 0:
                    pool.wait_ge(dest_ready, 2 * s + 2)
                pool.sem_inc(scatter_go, 1)
                for j in range(tiles):
                    g.indirect_dma_start(
                        out=scratch["y"].rearrange("r (h c) -> (r h) c", h=2),
                        out_offset=bass.IndirectOffsetOnAxis(ap=dest[:, j, half:half + 1], axis=0),
                        in_=y[:, j, :], in_offset=None).then_inc(y_out, 16 if j < tiles - 1 else 16 * (ST - tiles + 1))

            def activate(s, width, pair):
                for f in range(FB * pair, FB * pair + FB):
                    pool.wait_ge(sig_ready, NF * s + f + 1)
                    g.tensor_tensor(gate[:, f % 4, 0:width], gate[:, f % 4, 0:width], sig[f % 2][:, 0:width], ALU.mult
                                    ).then_inc(swish_ready, 1)
                for f in range(FB * pair, FB * pair + FB):
                    pool.wait_ge(swish_ready, OPEN + NF * s + f + 1)
                    pool.wait_ge(up_ready, OPEN + NF * s + f + 1)
                    g.tensor_tensor(up[f % 2][:, 0:width], gate[:, f % 4, 0:width], up[f % 2][:, 0:width], ALU.mult
                                    ).then_inc(act_ready, 1)

            def first_half(s, width):
                for pair in range(2):
                    activate(s, width, pair)

            def rest(s, width):
                for pair in range(2, 4):
                    activate(s, width, pair)
                for half in range(2):
                    scatter(s, half, tile_count(width))

            for opened in (swish_ready, act_ready):
                pool.sem_inc(opened, OPEN)
            for_first_slot(pool, keep, gather)
            pool.dma_start(bgu[:], io["b_gate_up"]).then_inc(y_out, OPEN_DMA)
            over_slots(pool, keep, (0, TILE_CLASS, TILE_WIDTHS, first_half),
                       (1, TILE_CLASS, TILE_WIDTHS, lambda s, width: gather(s + 1, width)),
                       (0, TILE_CLASS, TILE_WIDTHS, rest))

        @block.tensor
        def _(pe):
            def turn(s, width, base):
                pe.wait_ge(x_in, 16 * ST * s + 16 * ST)
                n = per_bank(width)
                for b in range(KD // n):
                    wait(pe, bank_free, base + b + 1 - BANKS)
                    for k in range(n * b, n * b + n):
                        for j in range(tile_count(width)):
                            c0 = (k - n * b) * width + j * P
                            ins = pe.transpose(ring[b % BANKS][:, c0:c0 + P], xg[:, j, k * P:(k + 1) * P],
                                               keep["ident"][:])
                    ins.then_inc(bank_full, n)

            def gate_up(s, width):
                with pe.Fori(0, 2) as half:
                    pe.wait_ge(bank_free, KD + USES * s)
                    for q in range(4):
                        pe.wait_ge(w_lo, OPEN + PIECES * s + 4 * half + q + 1)
                        piece = w[q % BUFFERS][:].rearrange("p a (k n) -> p a k n", n=FB * P)
                        for i in range(FB):
                            use = KD + USES * s + 4 * FB * half + FB * q + i
                            pe.wait_ge(bank_free, use + 1 - BANKS)
                            m = 0
                            for k in range(KD):
                                for a, b in SPLIT3:
                                    ins = pe.matmul(ring[(FB * q + i) % BANKS][:, 0:width],
                                                    piece[:, a, k, i * P:(i + 1) * P],
                                                    xT[:, b, k, 0:width], start=(m == 0), stop=(m == 3 * KD - 1))
                                    m += 1
                            ins.then_inc(bank_full, 1)

            def down(s, width, q):
                tiles = tile_count(width)
                dh, fh = divmod(q - 8, 2)
                pe.wait_ge(act_lo, OPEN + NF * s + FH * (fh + 1))
                pe.wait_ge(w_lo, OPEN + PIECES * s + q + 1)
                piece = w[q % BUFFERS][:].rearrange("p a (k n) -> p a k n", n=HALF)
                for j in range(tiles):
                    if fh == 0:
                        pe.wait_ge(y_free, OPEN + 2 * ST * s + (j + 1 if dh else 0))
                    m = 0
                    for f in range(FH):
                        for a, b in SPLIT3:
                            ins = pe.matmul(psY[j][:], actT[:, a, FH * fh + f, j * P:(j + 1) * P], piece[:, b, f, :],
                                            start=(fh == 0 and m == 0), stop=(fh == 1 and m == 3 * FH - 1))
                            m += 1
                    ins.then_inc(y_full, 1 if j < tiles - 1 else ST - tiles + 1)

            def before_turn(s, width):
                gate_up(s, width)
                for q in range(8, TURN):
                    down(s, width, q)

            def after_turn(s, width):
                for q in range(TURN, PIECES):
                    down(s, width, q)

            pe.sem_inc(y_full, OPEN)
            pe.wait_ge(banks_zeroed, 1)
            for_first_slot(pe, keep, lambda s, width: turn(s, width, 0))
            over_slots(pe, keep, (0, PE_CLASS, PE_WIDTHS, before_turn),
                       (1, TILE_CLASS, TILE_WIDTHS, lambda s, width: turn(s + 1, width, KD + USES * s + 2 * KD)),
                       (0, TILE_CLASS, TILE_WIDTHS, after_turn))

        @block.scalar
        def _(act):
            def split_hi(s, q):
                r = q % BUFFERS
                act.wait_ge(raw_in[r], 16 * (PIECES // BUFFERS) * s + 16 * (q // BUFFERS) + 16)
                if q >= BUFFERS:
                    act.wait_ge(*piece_done(s, q - BUFFERS))
                elif q == BUFFERS - 1:
                    act.wait_ge(y_full, OPEN + 4 * ST * s)
                nc.scalar.copy(w[r][:, 0, :], raw[r][:]).then_inc(w_hi, 1)

            def x_high(s, width):
                n = per_bank(width)
                for b in range(KD // n):
                    act.wait_ge(bank_full, USES * s + n * b + n)
                    nc.scalar.copy(xT[:, 0, n * b:n * b + n, 0:width], turned(b, width)).then_inc(x_hi, n)

            def before_turn(s, width):
                for q in range(8):
                    split_hi(s, q + 3)
                    for i in range(FB):
                        f = FB * (q // 2) + i
                        n = NF * s + f
                        if q % 2 == 0:
                            act.wait_ge(bank_free, KD + USES * s + FB * q + i + 1)
                            act.wait_ge(swish_ready, OPEN + (NF * s if f < 2 else n - 1))
                            nc.scalar.activation(sig[f % 2][:, 0:width], gate[:, f % 4, 0:width], ACT.Sigmoid,
                                                 scale=ALPHA).then_inc(sig_ready, 1)
                        else:
                            act.wait_ge(act_ready, OPEN + n + 1)
                            if f == 0:
                                act.wait_ge(y_full, OPEN + 4 * ST * s)
                            nc.scalar.copy(actT[:, 0, f, 0:width], up[f % 2][:, 0:width]).then_inc(act_hi, 1)

                copy_out(s, width, range(8, TURN))

            def copy_out(s, width, pieces):
                tiles = tile_count(width)
                for q in pieces:
                    split_hi(s, q + 3)
                    dh, fh = divmod(q - 8, 2)
                    if fh == 1:
                        act.wait_ge(y_out, OPEN_DMA + 16 * ST * (2 * s + dh))
                        for j in range(tiles):
                            act.wait_ge(y_full, OPEN + 4 * ST * s + ST * (q - 8) + j + 1)
                            nc.scalar.copy(y[:, j, :], psY[j][:]
                                           ).then_inc(y_free, 1 if j < tiles - 1 else ST - tiles + 1)

            act.sem_inc(y_free, OPEN)
            for q in range(BUFFERS - 1):
                act.wait_ge(raw_in[q], 16)
                nc.scalar.copy(w[q][:, 0, :], raw[q][:]).then_inc(w_hi, 1)
            for_first_slot(act, keep, x_high)
            over_slots(act, keep, (0, TILE_CLASS, TILE_WIDTHS, before_turn),
                       (1, TILE_CLASS, TILE_WIDTHS, lambda s, width: x_high(s + 1, width)),
                       (0, TILE_CLASS, TILE_WIDTHS, lambda s, width: copy_out(s, width, range(TURN, PIECES))))
            act.wait_ge(y_out, table_entry(act, keep, 0, USED, NSLOTS) * (32 * ST) + OPEN_DMA)
            act.sem_inc(all_stored, 1)

        @block.vector
        def _(dve):
            v = nc.vector

            def list_tokens(s):
                v.tensor_copy(idx[:], keep["tokens"][:, bass.ds(ST * s, ST)]).then_inc(idx_ready, 1)

            def split_lo(s, q):
                r = q % BUFFERS
                dve.wait_ge(w_hi, PIECES * s + q + 1)
                v.tensor_tensor(w[r][:, 1, :], raw[r][:], w[r][:, 0, :].bitcast(F32), ALU.subtract
                                ).then_inc(w_lo, 1)

            def x_low(s, width):
                n = per_bank(width)
                for b in range(KD // n):
                    dve.wait_ge(x_hi, KD * s + n * b + n)
                    v.tensor_tensor(xT[:, 1, n * b:n * b + n, 0:width], turned(b, width),
                                    xT[:, 0, n * b:n * b + n, 0:width].bitcast(F32), ALU.subtract
                                    ).then_inc(bank_free, n)

            def act_low(s, f, width):
                r = f % 2
                dve.wait_ge(act_hi, NF * s + f + 1)
                v.tensor_tensor(actT[:, 1, f, 0:width], up[r][:, 0:width], actT[:, 0, f, 0:width].bitcast(F32),
                                ALU.subtract).then_inc(act_lo, 1)

            def before_turn(s, width):
                e = table_entry(dve, keep, s, EXPERT, E - 1)
                dve.wait_ge(up_ready, OPEN + NF * s)
                v.tensor_copy(bias[:].unsqueeze(1), bgu[:, bass.ds(e, 1), :]).then_inc(bias_ready, 1)
                dve.wait_ge(bias_ready, s + 1)
                for q in range(8):
                    if q == 1:
                        dve.wait_ge(x_in, 16 * ST * s + 16 * ST)
                        list_tokens(s + 1)
                    if q == 2:
                        dve.wait_ge(y_out, OPEN_DMA + 32 * ST * s)
                        v.tensor_copy(dest[:, :, 0], keep["targets"][:, bass.ds(ST * s, ST)]).then_inc(dest_ready, 1)
                        dve.wait_ge(dest_ready, 2 * s + 1)
                        v.tensor_scalar(dest[:, :, 1], dest[:, :, 0], 1.0, None, ALU.add).then_inc(dest_ready, 1)
                    for i in range(FB):
                        f = FB * (q // 2) + i
                        n = NF * s + f
                        use = KD + USES * s + FB * q + i
                        bank = ring[(FB * q + i) % BANKS]
                        dve.wait_ge(bank_full, use + 1)
                        if q % 2 == 0:
                            dve.wait_ge(act_ready, OPEN + (n - 3 if f > 3 else NF * s))
                            v.tensor_scalar(gate[:, f % 4, 0:width], bank[:, 0:width], bias[:, f:f + 1], LIMIT,
                                            ALU.add, ALU.min).then_inc(bank_free, 1)
                        else:
                            if f >= 2:
                                act_low(s, f - 2, width)
                            dve.wait_ge(act_lo, OPEN + (n - 1 if f >= 2 else NF * s))
                            v.tensor_scalar(up[f % 2][:, 0:width], bank[:, 0:width], bias[:, NF + f:NF + f + 1], -LIMIT,
                                            ALU.add, ALU.max).then_inc(bank_free, 1)
                            dve.wait_ge(bank_free, use + 1)
                            v.tensor_scalar(up[f % 2][:, 0:width], up[f % 2][:, 0:width], LIMIT, 1.0,
                                            ALU.min, ALU.add).then_inc(up_ready, 1)
                    if q < 7:
                        split_lo(s, q + 3)
                act_low(s, NF - 2, width)
                act_low(s, NF - 1, width)
                for q in range(7, TURN):
                    split_lo(s, q + 3)

            def after_turn(s, width):
                for q in range(TURN, PIECES):
                    split_lo(s, q + 3)

            for opened in (w_lo, up_ready, act_lo):
                dve.sem_inc(opened, OPEN)
            list_tokens(0)
            for b in range(BANKS):
                last = v.memset(ring[b][:], 0.0)
            last.then_inc(banks_zeroed, 1)
            for q in range(BUFFERS - 1):
                split_lo(0, q)
            for_first_slot(dve, keep, x_low)
            dve.wait_ge(y_out, OPEN_DMA)
            over_slots(dve, keep, (0, TILE_CLASS, TILE_WIDTHS, before_turn),
                       (1, TILE_CLASS, TILE_WIDTHS, lambda s, width: x_low(s + 1, width)),
                       (0, TILE_CLASS, TILE_WIDTHS, after_turn))


def combine_stage(nc, io, scratch, keep, out):
    with ExitStack() as ctx:
        sb = lambda s, shape, dt=F32: ctx.enter_context(nc.sbuf_tensor(f"co_{s}", shape, dt))
        ps = lambda s, shape: ctx.enter_context(nc.psum_tensor(f"co_ps_{s}", shape, F32))
        sem = stage_semaphores(nc, ctx, "co")
        y4 = [sb(f"y{p}", [P, TOPK, D]) for p in range(2)]
        ht = [sb(f"h{p}", [P, D]) for p in range(2)]
        own = [sb(f"own{p}", [P, E]) for p in range(2)]
        ownT, down_bias = sb("ownT", [E, P]), sb("down_bias", [E, D])
        acc = [sb(f"acc{p}", [P, D]) for p in range(2)]
        squares, scaled = sb("squares", [P, D]), sb("scaled", [P, D])
        stat, work = sb("stat", [P, 2, 2]), sb("work", [P, ROOT_WORK, 1])
        gains = sb("gains", [P, D])
        result = [sb(f"result{p}", [P, D]) for p in range(2)]
        psT = ps("t", [E, P])
        psB = [ps(f"b{n}", [P, W]) for n in range(2)]

        y_in, h_in, result_out = ([sem(f"{s}{p}") for p in range(2)] for s in ("y_in", "h_in", "result_out"))
        bias_in, gains_in = sem("bias_in"), sem("gains_in")
        own_ready, own_turned, ownT_ready, bias_done = (sem(s) for s in ("own_ready", "own_turned", "ownT_ready", "bias_done"))
        sums, squares_ready, root_steps, rstd_ready = (sem(s) for s in ("sums", "squares_ready", "root_steps", "rstd_ready"))
        scaled_ready, result_ready = sem("scaled_ready"), sem("result_ready")
        SUMS = 2 + TOPK
        block = ctx.enter_context(nc.Block())

        @block.sync
        def _(sp):
            def store(tile):
                sp.wait_ge(result_ready, tile.t + 1)
                sp.dma_start(out[tile.rows, :], result[tile.p][:]).then_inc(result_out[tile.p], 16)

            def body(tile):
                wait(sp, sums, SUMS * (tile.t - 1))
                sp.dma_start(ht[tile.p][:], scratch["h"][tile.rows, :]).then_inc(h_in[tile.p], 16)
                sp.dma_start(y4[tile.p][:].rearrange("p k d -> p (k d)"), scratch["y"][
                    bass.ds(tile.t * P * TOPK, P * TOPK), :].rearrange("(p k) d -> p (k d)", k=TOPK)
                    ).then_inc(y_in[tile.p], 16)
                if tile.has(-2):
                    store(tile.at(-2))

            sp.dma_start(down_bias[:], io["b_down"]).then_inc(bias_in, 16)
            sp.dma_start(gains[:], io["normf_g"].to_broadcast([P, D])).then_inc(gains_in, 16)
            over_tiles(sp, body)
            store(Tile(T // 2 - 1, 0))
            store(Tile(T // 2 - 1, 1))
            for p in range(2):
                sp.wait_ge(result_out[p], 16 * (T // 2))

        @block.gpsimd
        def _(pool):
            def finish(tile):
                pool.wait_ge(scaled_ready, tile.t + 1)
                wait(pool, result_out[tile.p], 16 * tile.i)
                nc.gpsimd.tensor_tensor(result[tile.p][:], scaled[:], gains[:], ALU.mult).then_inc(result_ready, 1)

            pool.wait_ge(gains_in, 16)
            over_tiles(pool, finish)

        @block.tensor
        def _(pe):
            def body(tile):
                pe.wait_ge(own_ready, tile.t + 1)
                wait(pe, ownT_ready, tile.t)
                pe.transpose(psT[:], own[tile.p][:], keep["ident"][:]).then_inc(own_turned, 1)
                pe.wait_ge(ownT_ready, tile.t + 1)
                wait(pe, sums, SUMS * tile.t - TOPK)
                for n in range(2):
                    ins = pe.matmul(psB[n][:], ownT[:], down_bias[:, n * W:(n + 1) * W], start=True, stop=True)
                ins.then_inc(bias_done, 1)
            pe.wait_ge(bias_in, 16)
            over_tiles(pe, body)

        @block.scalar
        def _(act):
            def keep_own(tile):
                act.wait_ge(own_turned, tile.t + 1)
                wait(act, bias_done, tile.t)
                nc.scalar.copy(ownT[:], psT[:]).then_inc(ownT_ready, 1)

            def square(tile):
                act.wait_ge(sums, SUMS * tile.t + SUMS)
                nc.scalar.activation(squares[:], acc[tile.p][:], ACT.Square, accum_out=stat[:, tile.p, 0:1]
                                     ).then_inc(squares_ready, 1)

            def scale(tile):
                act.wait_ge(rstd_ready, tile.t + 1)
                wait(act, result_ready, tile.t)
                nc.scalar.mul(scaled[:], acc[tile.p][:], stat[:, tile.p, 1:2]).then_inc(scaled_ready, 1)

            def body(tile):
                if tile.has(-1):
                    square(tile.at(-1))
                if tile.has(1):
                    keep_own(tile.at(1))
                if tile.has(-1):
                    scale(tile.at(-1))

            keep_own(Tile(0, 0))
            over_tiles(act, body)
            square(Tile(T // 2 - 1, 1))
            scale(Tile(T // 2 - 1, 1))

        @block.vector
        def _(dve):
            v = nc.vector

            def own_gates(tile):
                wait(dve, own_turned, tile.t - 1)
                v.tensor_copy(own[tile.p][:].unsqueeze(1), keep["spread"][:, bass.ds(tile.t, 1), :]
                              ).then_inc(own_ready, 1)

            def body(tile):
                p, t = tile.p, tile.t
                c = Chain(dve, sums, SUMS * t)
                if tile.has(1):
                    own_gates(tile.at(1))
                dve.wait_ge(h_in[p], 16 * tile.i + 16)
                dve.wait_ge(bias_done, t + 1)
                wait(dve, scaled_ready, t - 1)
                v.tensor_tensor(acc[p][:, 0:W], psB[0][:], ht[p][:, 0:W], ALU.add).then_inc(sums, 1)
                v.tensor_tensor(acc[p][:, W:D], psB[1][:], ht[p][:, W:D], ALU.add).then_inc(sums, 1)
                c.n = 2
                dve.wait_ge(sums, SUMS * t + 2)
                dve.wait_ge(y_in[p], 16 * tile.i + 16)
                for k in range(TOPK):
                    c.then(v.scalar_tensor_tensor(
                        acc[p][:], y4[p][:, k, :], keep["gates"][:, bass.ds(t, 1), k:k + 1].rearrange("p a b -> p (a b)"),
                        acc[p][:], ALU.mult, ALU.add))
                    if k == 0 and tile.has(-1):
                        root(tile.at(-1))

            def root(tile):
                p, t = tile.p, tile.t
                dve.wait_ge(squares_ready, t + 1)
                inverse_root(nc, Chain(dve, root_steps, ROOT_STEPS * t), 1.0 / D, stat[:, p, 0:1], work[:],
                             stat[:, p, 1:2]).then_inc(rstd_ready, 1)
                dve.wait_ge(rstd_ready, t + 1)

            own_gates(Tile(0, 0))
            over_tiles(dve, body)
            root(Tile(T // 2 - 1, 1))


def decoder_block(nc, io, out, last="combine"):
    scratch = {
        "a": nc.dram_tensor("a_out", (S, W), F32).ap(),
        "v": nc.dram_tensor("values", (S, W), F32).ap(),
        "o": nc.dram_tensor("branches", (3, S, OROW), F32).ap(),
        "h": nc.dram_tensor("hidden", (S, D), F32).ap(),
        "hn": nc.dram_tensor("hidden_scaled", (S, D), F32).ap(),
        "y": nc.dram_tensor("expert_rows", (S * TOPK + COLS * P, D), F32).ap(),
        "table": nc.dram_tensor("slot_table", (NSLOTS + 1, ENTRY), I32).ap(),
    }
    with ExitStack() as ctx:
        keep = {
            "ident": ctx.enter_context(nc.sbuf_tensor("ident", [P, P], F32)),
            "ident_in": ctx.enter_context(nc.semaphore("ident_in")),
        }
        for name, shape, dt in (("tokens", [P, COLS], U32), ("targets", [P, COLS], U32), ("gates", [P, T, TOPK], F32),
                                ("spread", [P, T, E], F32), ("table", [1, ENTRY * (NSLOTS + 1)], I32)):
            keep[name] = ctx.enter_context(nc.sbuf_tensor(name, shape, dt))
        with nc.Block() as block:
            @block.sync
            def _(sp):
                sp.dma_start(keep["ident"][:], io["ident"]).then_inc(keep["ident_in"], 16)
        gating_stage(nc, io, scratch, keep)
        with ExitStack() as heads:
            for name in ("qT", "kT"):
                keep[name] = heads.enter_context(nc.sbuf_tensor(name, [P, PAIRS, S], F32))
            rotary_stage(nc, io, scratch, keep)
            attention_stage(nc, io, scratch, keep)
        if last == "attention":
            return
        with nc.sbuf_tensor("logits", [P, T, E], F32) as keep["logits"]:
            mixing_stage(nc, io, scratch, keep)
            if last == "mixing":
                return
            routing_stage(nc, io, scratch, keep)
        if last == "routing":
            return
        experts_stage(nc, io, scratch, keep)
        combine_stage(nc, io, scratch, keep, out)


_LAYOUT = {
    "x": lambda a: a.reshape(S, D),
    "norm1_g": lambda a: a.reshape(KD, P).T,
    "w_in": lambda a: a.reshape(D, -1),
    "a_ln_g": lambda a: a.reshape(1, W),
    "a_ln_b": lambda a: a.reshape(1, W),
    "a_w_s": lambda a: a.reshape(H, P, P).transpose(2, 0, 1),
    "a_b_s": lambda a: a.reshape(H, P).T,
    "w_out": lambda a: a.reshape(D, D),
    "norm2_g": lambda a: a.reshape(1, D),
    "w_router": lambda a: a.reshape(KD, P, E).transpose(1, 0, 2),
    "b_router": lambda a: a.reshape(1, E),
    "w_gate_up": lambda a: a.reshape(E, D, 2 * FF),
    "b_gate_up": lambda a: a.reshape(E, 2 * FF // P, P).transpose(2, 0, 1),
    "w_down": lambda a: a.reshape(E, FF, D),
    "b_down": lambda a: a.reshape(E, D),
    "normf_g": lambda a: a.reshape(1, D),
}


def _constants():
    import numpy as np
    f = np.float32
    inv = f(10000.0) ** (-np.arange(0, DH, 2, dtype=f) / f(DH))
    angle = np.arange(S, dtype=f)[:, None] * inv[None, :]
    cos, sin = np.cos(angle), np.sin(angle)
    at = np.arange(P)
    before, here = at[None, :] < at[:, None], at[None, :] > at[:, None]
    band = np.where(np.concatenate([before, here], 1), f(-1e30), f(0))
    return {
        "ident": np.eye(P, dtype=f),
        "rope": np.stack([np.concatenate([cos, cos], 1), np.concatenate([-sin, sin], 1)], 1).astype(f),
        "tri": (at[:, None] <= at[None, :]).astype(f),
        "before": (at[:, None] < at[None, :]).astype(f),
        "band": band.astype(f),
        "token_mark": (np.arange(T)[None, :] * P + at[:, None] + 1).astype(f),
        "column": np.arange(COLS, dtype=f)[None, :],
        "expert": np.arange(E, dtype=f)[None, :],
        "slot": np.arange(P, dtype=f)[:, None],
    }


def kernel(**inputs):
    import numpy as np
    import concourse.bacc as bacc
    from concourse.bass_utils import run_bass_kernel_spmd

    nc = bacc.Bacc("TRN2", target_bir_lowering=False, num_devices=1)
    arrays = {name: np.ascontiguousarray(lay(np.asarray(inputs[name]))) for name, lay in _LAYOUT.items()}
    gains = np.concatenate([np.asarray(inputs["a_out_g"]).reshape(W), np.asarray(inputs["b_out_g"]).reshape(W)])
    arrays["mix_g"] = np.ascontiguousarray(gains.reshape(KD, P).T)
    arrays.update(_constants())
    io = {name: nc.dram_tensor(f"in_{name}", a.shape, mybir.dt.from_np(a.dtype), kind="ExternalInput").ap()
          for name, a in arrays.items()}
    out = nc.dram_tensor("out", (S, D), F32, kind="ExternalOutput").ap()
    decoder_block(nc, io, out)
    done = run_bass_kernel_spmd(nc, [{f"in_{name}": a for name, a in arrays.items()}], core_ids=[0])
    return done.results[0]["out"].reshape(1, S, D)
```
